# Optimizing a Trainium2 kernel written in Bass

```python
import math
import jax
import jax.numpy as jnp
from jax import lax
import numpy as np

D_MODEL = 1024
BATCH = 1
SEQ = 512
DEPTH = 2

GRID_W = 64
CTX_LEN = 256

NA_HEADS = 8
NA_DIM = 64
NA_W = NA_HEADS * NA_DIM
WIN_R = 8
WIN_C = 16
NA_QCB = 16
NA_KCS = 32

DN_HEADS = 8
DN_DK = 64
DN_DV = 64
DN_KW = DN_HEADS * DN_DK
DN_VW = DN_HEADS * DN_DV
DN_CHUNK = 64

SSD_HEADS = 16
SSD_P = 64
SSD_GROUPS = 2
SSD_N = 128
SSD_DI = SSD_HEADS * SSD_P
SSD_BC = SSD_GROUPS * SSD_N
SSD_XBC = SSD_DI + 2 * SSD_BC
SSD_CHUNK = 64

CONV_W = 5
D_FF = 4 * D_MODEL
ROPE_THETA = 10000.0
EPS = 1e-6

IN_SPLITS = (3 * NA_W, 2 * DN_KW + DN_VW, DN_VW, 2 * DN_HEADS, 2 * DN_HEADS,
             SSD_DI, SSD_XBC, 2 * SSD_HEADS, 3 * D_MODEL)
D_IN = sum(IN_SPLITS)

F32 = jnp.float32

kernel_name = 'hybrid_na_gdn_ssd_dit_block'

def rms_norm(x, gain):
    xf = x.astype(F32)
    y = xf * lax.rsqrt(jnp.mean(xf * xf, axis=-1, keepdims=True) + EPS)
    return (y * gain.astype(F32)).astype(x.dtype)

def l2_norm(x):
    xf = x.astype(F32)
    return xf * lax.rsqrt(jnp.sum(xf * xf, axis=-1, keepdims=True) + EPS)

def modulate(x, shift, scale):
    return x * (1.0 + scale) + shift

def _flip(t):
    return None if t is None else jnp.flip(t, axis=1)

def dwconv_centred(x, w, b=None):
    y = lax.conv_general_dilated(
        x, w[:, None, :].astype(x.dtype), window_strides=(1,),
        padding=[(CONV_W // 2, CONV_W // 2)],
        dimension_numbers=('NWC', 'WIO', 'NWC'), feature_group_count=x.shape[-1])
    return y if b is None else y + b.astype(y.dtype)

def axial_rope(x):
    seq_len, dh = x.shape[1], x.shape[-1]
    half, quarter = dh // 2, dh // 4
    pos = jnp.arange(seq_len)
    inv_freq = ROPE_THETA ** (-jnp.arange(quarter, dtype=F32) / quarter)

    def rotate(xa, p):
        ang = p.astype(F32)[:, None] * inv_freq
        cos, sin = jnp.cos(ang)[None, :, None, :], jnp.sin(ang)[None, :, None, :]
        x1, x2 = xa[..., :quarter], xa[..., quarter:]
        return jnp.concatenate([x1 * cos - x2 * sin, x1 * sin + x2 * cos], axis=-1)

    return jnp.concatenate([rotate(x[..., :half], pos // GRID_W),
                            rotate(x[..., half:], pos % GRID_W)], axis=-1)

def split_cols(u):
    return jnp.split(u, [int(i) for i in np.cumsum(IN_SPLITS)[:-1]], axis=-1)

def neighbourhood_attention(qkv, qkv_c, q_gain, k_gain, rpb, need_ctx):
    bsz, seq_len, _ = qkv.shape
    ctx_len = qkv_c.shape[1]
    t = qkv.reshape(bsz, seq_len, 3, NA_HEADS, NA_DIM)
    tc = qkv_c.reshape(bsz, ctx_len, 3, NA_HEADS, NA_DIM)
    scale = NA_DIM ** -0.5
    q = rms_norm(t[:, :, 0], q_gain) * scale
    k = rms_norm(t[:, :, 1], k_gain)
    v = t[:, :, 2]
    kc = rms_norm(tc[:, :, 1], k_gain)
    vc = tc[:, :, 2]

    rows = seq_len // GRID_W
    wr = min(WIN_R, rows)
    ncb = GRID_W // NA_QCB
    r = np.arange(rows)
    row_idx = np.clip(r - wr // 2, 0, rows - wr)[:, None] + np.arange(wr)
    qcol = np.arange(ncb)[:, None] * NA_QCB + np.arange(NA_QCB)
    kcol = (np.clip(np.arange(ncb) * NA_QCB - WIN_C // 2, 0, GRID_W - NA_KCS)[:, None]
            + np.arange(NA_KCS))
    wstart = np.clip(qcol - WIN_C // 2, 0, GRID_W - WIN_C)
    col_ok = (kcol[:, None, :] >= wstart[..., None]) & (kcol[:, None, :] < wstart[..., None] + WIN_C)
    dr = row_idx - r[:, None] + (WIN_R - 1)
    dc = np.clip(kcol[:, None, :] - qcol[..., None], 1 - WIN_C, WIN_C - 1) + (WIN_C - 1)
    bias = rpb.astype(F32)[:, dr[None, :, None, :, None], dc[:, None, :, None, :]]
    bias = jnp.where(col_ok[:, None, :, None, :], bias, -jnp.inf)
    bias = jnp.moveaxis(bias, 0, 1)

    q_blocks = jnp.moveaxis(q.reshape(bsz, rows, ncb, NA_QCB, NA_HEADS, NA_DIM), 2, 0)
    k_grid = k.reshape(bsz, rows, GRID_W, NA_HEADS, NA_DIM)
    v_grid = v.reshape(bsz, rows, GRID_W, NA_HEADS, NA_DIM)
    row_idx_j = jnp.asarray(row_idx)
    n_win = wr * NA_KCS

    def query_block(args):
        qb, kcol_b, bias_b = args
        kb = jnp.take(k_grid, kcol_b, axis=2)[:, row_idx_j]
        vb = jnp.take(v_grid, kcol_b, axis=2)[:, row_idx_j].reshape(bsz, rows, n_win, NA_HEADS, NA_DIM)
        s_win = jnp.einsum('brqhd,brwkhd->bhrqwk', qb, kb).astype(F32) + bias_b[None]
        s_ctx = jnp.einsum('brqhd,bmhd->bhrqm', qb, kc).astype(F32)
        s = jnp.concatenate([s_win.reshape(bsz, NA_HEADS, rows, NA_QCB, n_win), s_ctx], axis=-1)
        p = jax.nn.softmax(s, axis=-1).astype(v.dtype)
        return (jnp.einsum('bhrqn,brnhd->brqhd', p[..., :n_win], vb)
                + jnp.einsum('bhrqm,bmhd->brqhd', p[..., n_win:], vc))

    o = lax.map(query_block, (q_blocks, jnp.asarray(kcol), bias))
    y = jnp.moveaxis(o, 0, 2).reshape(bsz, seq_len, NA_W)

    yc = None
    if need_ctx:
        qc = rms_norm(tc[:, :, 0], q_gain) * scale
        pc = jax.nn.softmax(jnp.einsum('bmhd,bnhd->bhmn', qc, kc).astype(F32), axis=-1).astype(vc.dtype)
        yc = jnp.einsum('bhmn,bnhd->bmhd', pc, vc).reshape(bsz, ctx_len, NA_W)
    return y, yc

def gdn_chunked(q, k, v, g, beta, s0, with_output):
    bsz, seq_len, n_h, _ = k.shape
    dv = v.shape[-1]
    cl = DN_CHUNK
    nc = seq_len // cl

    def chunks(t):
        return jnp.swapaxes(t.astype(F32).reshape(bsz, nc, cl, n_h, *t.shape[3:]), 2, 3)

    k, v, g, beta = chunks(k), chunks(v), chunks(g), chunks(beta)
    incl = np.tril(np.ones((cl, cl), dtype=bool))
    strict = np.tril(np.ones((cl, cl), dtype=bool), -1)
    gam = jnp.cumsum(g, axis=-1)
    dec = jnp.exp(jnp.where(incl, gam[..., :, None] - gam[..., None, :], -jnp.inf))
    kb = k * beta[..., None]
    a = jnp.where(strict, jnp.einsum('bnhid,bnhjd->bnhij', kb, k) * dec, 0.0)
    eye = jnp.eye(cl, dtype=F32)
    tmat = lax.linalg.triangular_solve(eye + a, jnp.broadcast_to(eye, a.shape),
                                       left_side=True, lower=True, unit_diagonal=True)
    u = tmat @ (v * beta[..., None])
    w = tmat @ (kb * jnp.exp(gam)[..., None])
    gam_last = gam[..., -1]
    kdec = k * jnp.exp(gam_last[..., None] - gam)[..., None]
    xs = [u, w, kdec, gam_last]
    if with_output:
        q = chunks(q)
        xs += [q * jnp.exp(gam)[..., None], jnp.einsum('bnhid,bnhjd->bnhij', q, k) * dec]

    def step(s, inp):
        v_new = inp[0] - inp[1] @ s
        s_next = s * jnp.exp(inp[3])[..., None, None] + jnp.swapaxes(inp[2], -1, -2) @ v_new
        if with_output:
            return s_next, inp[4] @ s + inp[5] @ v_new
        return s_next, None

    s_fin, o = lax.scan(step, s0.astype(F32), [jnp.moveaxis(t, 1, 0) for t in xs])
    if with_output:
        o = jnp.swapaxes(jnp.moveaxis(o, 0, 1), 2, 3).reshape(bsz, seq_len, n_h, dv)
    return o, s_fin

def _gdn_inputs(qkv_s, b_s, a_s, conv_w, a_log, dt_bias, use_rope, need_q):
    bsz, n, _ = qkv_s.shape
    t = jax.nn.silu(dwconv_centred(qkv_s, conv_w)).astype(F32)
    q, k, v = jnp.split(t, [DN_KW, 2 * DN_KW], axis=-1)
    k = l2_norm(k.reshape(bsz, n, DN_HEADS, DN_DK))
    if use_rope:
        k = axial_rope(k)
    if need_q:
        q = l2_norm(q.reshape(bsz, n, DN_HEADS, DN_DK))
        if use_rope:
            q = axial_rope(q)
        q = q * DN_DK ** -0.5
    else:
        q = None
    v = v.reshape(bsz, n, DN_HEADS, DN_DV)
    beta = jax.nn.sigmoid(b_s.astype(F32)).reshape(bsz, n, 2, DN_HEADS)
    g = -jnp.exp(a_log.astype(F32)) * jax.nn.softplus(
        a_s.astype(F32).reshape(bsz, n, 2, DN_HEADS) + dt_bias.astype(F32))
    return q, k, v, beta, g

def gated_deltanet(qkv, z, b_raw, a_raw, qkv_c, z_c, b_raw_c, a_raw_c,
                   conv_w, a_log, dt_bias, o_gain, need_ctx):
    bsz = qkv.shape[0]
    q, k, v, beta, g = _gdn_inputs(qkv, b_raw, a_raw, conv_w, a_log, dt_bias, True, True)
    qc, kc, vc, betac, gc = _gdn_inputs(qkv_c, b_raw_c, a_raw_c, conv_w, a_log, dt_bias, False, need_ctx)
    s0 = jnp.zeros((bsz, DN_HEADS, DN_DK, DN_DV), F32)
    oc_f, sc_f = gdn_chunked(qc, kc, vc, gc[:, :, 0], betac[:, :, 0], s0, need_ctx)
    oc_b, sc_b = gdn_chunked(_flip(qc), _flip(kc), _flip(vc), _flip(gc[:, :, 1]), _flip(betac[:, :, 1]), s0, need_ctx)
    o_f, _ = gdn_chunked(q, k, v, g[:, :, 0], beta[:, :, 0], sc_f, True)
    o_b, _ = gdn_chunked(_flip(q), _flip(k), _flip(v), _flip(g[:, :, 1]), _flip(beta[:, :, 1]), sc_b, True)

    def gated_out(o, zs):
        n = zs.shape[1]
        zh = zs.astype(F32).reshape(bsz, n, DN_HEADS, DN_DV)
        return (rms_norm(o, o_gain) * jax.nn.silu(zh)).reshape(bsz, n, DN_VW)

    y = gated_out(o_f + _flip(o_b), z)
    yc = gated_out(oc_f + _flip(oc_b), z_c) if need_ctx else None
    return y, yc

def ssd_chunked(xs, dt, a, bm, cm, h0, with_output):
    bsz, seq_len, n_h, hp = xs.shape
    n_g, n_s = bm.shape[2], bm.shape[3]
    n_r = n_h // n_g
    cl = SSD_CHUNK
    nc = seq_len // cl
    x = xs.reshape(bsz, nc, cl, n_g, n_r, hp)
    dtc = dt.reshape(bsz, nc, cl, n_g, n_r)
    bc = bm.reshape(bsz, nc, cl, n_g, n_s)
    lam = jnp.cumsum(dtc * a.reshape(n_g, n_r), axis=2)
    lam_last = lam[:, :, -1]
    st = jnp.einsum('bcjgn,bcjgr,bcjgrp->bcgrpn', bc, jnp.exp(lam_last[:, :, None] - lam) * dtc, x)

    def step(h, inp):
        st_c, dec_c = inp
        h_next = h * jnp.exp(dec_c)[..., None, None] + st_c
        return h_next, (h if with_output else None)

    h_fin, h_prev = lax.scan(step, h0.reshape(bsz, n_g, n_r, hp, n_s),
                             (jnp.moveaxis(st, 1, 0), jnp.moveaxis(lam_last, 1, 0)))
    h_fin = h_fin.reshape(bsz, n_h, hp, n_s)
    if not with_output:
        return None, h_fin
    cc = cm.reshape(bsz, nc, cl, n_g, n_s)
    y_inter = jnp.einsum('bcign,bcigr,bcgrpn->bcigrp', cc, jnp.exp(lam), jnp.moveaxis(h_prev, 0, 1))
    incl = np.tril(np.ones((cl, cl), dtype=bool))
    lam_t = jnp.moveaxis(lam, 2, -1)
    dec = jnp.exp(jnp.where(incl, lam_t[..., :, None] - lam_t[..., None, :], -jnp.inf))
    cb = jnp.einsum('bcign,bcjgn->bcgij', cc, bc)
    wgt = cb[:, :, :, None] * dec * jnp.moveaxis(dtc, 2, -1)[..., None, :]
    y_intra = jnp.einsum('bcgrij,bcjgrp->bcigrp', wgt, x)
    return (y_inter + y_intra).reshape(bsz, seq_len, n_h, hp), h_fin

def _ssd_inputs(xbc_s, dt_s, conv_w, conv_b, dt_bias):
    bsz, n, _ = xbc_s.shape
    t = jax.nn.silu(dwconv_centred(xbc_s, conv_w, conv_b)).astype(F32)
    xs, bm, cm = jnp.split(t, [SSD_DI, SSD_DI + SSD_BC], axis=-1)
    dt = jax.nn.softplus(dt_s.astype(F32).reshape(bsz, n, 2, SSD_HEADS) + dt_bias.astype(F32))
    return (xs.reshape(bsz, n, SSD_HEADS, SSD_P), bm.reshape(bsz, n, SSD_GROUPS, SSD_N),
            cm.reshape(bsz, n, SSD_GROUPS, SSD_N), dt)

def mamba2_ssd(z, xbc, dt_raw, z_c, xbc_c, dt_raw_c, conv_w, conv_b, a_log, dt_bias,
               d_skip, o_gain, need_ctx):
    bsz = z.shape[0]
    a = -jnp.exp(a_log.astype(F32))
    xs, bm, cm, dt = _ssd_inputs(xbc, dt_raw, conv_w, conv_b, dt_bias)
    xsc, bmc, cmc, dtc = _ssd_inputs(xbc_c, dt_raw_c, conv_w, conv_b, dt_bias)
    h0 = jnp.zeros((bsz, SSD_HEADS, SSD_P, SSD_N), F32)
    yc_f, hc_f = ssd_chunked(xsc, dtc[:, :, 0], a[0], bmc, cmc, h0, need_ctx)
    yc_b, hc_b = ssd_chunked(_flip(xsc), _flip(dtc[:, :, 1]), a[1], _flip(bmc), _flip(cmc), h0, need_ctx)
    y_f, _ = ssd_chunked(xs, dt[:, :, 0], a[0], bm, cm, hc_f, True)
    y_b, _ = ssd_chunked(_flip(xs), _flip(dt[:, :, 1]), a[1], _flip(bm), _flip(cm), hc_b, True)

    def gated_out(ys, xss, zs):
        n = zs.shape[1]
        yy = (ys + d_skip.astype(F32)[:, None] * xss).reshape(bsz, n, SSD_DI) * jax.nn.silu(zs.astype(F32))
        grp = yy.reshape(bsz, n, SSD_GROUPS, SSD_DI // SSD_GROUPS)
        return rms_norm(grp, o_gain.reshape(SSD_GROUPS, SSD_DI // SSD_GROUPS)).reshape(bsz, n, SSD_DI)

    y = gated_out(y_f + _flip(y_b), xs, z)
    yc = gated_out(yc_f + _flip(yc_b), xsc, z_c) if need_ctx else None
    return y, yc

def token_mixer(h, hc, w_in, na_q_gain, na_k_gain, na_rpb, dn_conv_w, dn_a_log, dn_dt_bias, dn_o_gain,
                ssd_conv_w, ssd_conv_b, ssd_a_log, ssd_dt_bias, ssd_d, ssd_o_gain,
                w_pa, w_pb, w_pc, w_out, need_ctx):
    (na_qkv, dn_qkv, dn_z, dn_b, dn_a, ssd_z, ssd_xbc, ssd_dt, gate_raw) = split_cols(h @ w_in)
    (na_qkv_c, dn_qkv_c, dn_z_c, dn_b_c, dn_a_c, ssd_z_c, ssd_xbc_c, ssd_dt_c, gate_raw_c) = split_cols(hc @ w_in)
    y_a, yc_a = neighbourhood_attention(na_qkv, na_qkv_c, na_q_gain, na_k_gain, na_rpb, need_ctx)
    y_b, yc_b = gated_deltanet(dn_qkv, dn_z, dn_b, dn_a, dn_qkv_c, dn_z_c, dn_b_c, dn_a_c,
                               dn_conv_w, dn_a_log, dn_dt_bias, dn_o_gain, need_ctx)
    y_c, yc_c = mamba2_ssd(ssd_z, ssd_xbc, ssd_dt, ssd_z_c, ssd_xbc_c, ssd_dt_c, ssd_conv_w, ssd_conv_b,
                           ssd_a_log, ssd_dt_bias, ssd_d, ssd_o_gain, need_ctx)

    def merge(ya, yb, ycc, g_raw):
        dtype = g_raw.dtype
        gts = jax.nn.sigmoid(g_raw.astype(F32)).astype(dtype).reshape(*g_raw.shape[:2], 3, D_MODEL)
        m = (gts[:, :, 0] * (ya.astype(dtype) @ w_pa)
             + gts[:, :, 1] * (yb.astype(dtype) @ w_pb)
             + gts[:, :, 2] * (ycc.astype(dtype) @ w_pc))
        return m @ w_out

    y = merge(y_a, y_b, y_c, gate_raw)
    yc = merge(yc_a, yc_b, yc_c, gate_raw_c) if need_ctx else None
    return y, yc

def squared_relu_mlp(h, w1, w2):
    return jnp.square(jax.nn.relu(h @ w1)) @ w2

def setup_inputs(seed: int = 0) -> dict:
    key = jax.random.key(seed)
    keys = iter(jax.random.split(key, 32))

    def normal(shape, scale):
        return scale * jax.random.normal(next(keys), shape, F32)

    def gain(shape):
        return 1.0 + 0.02 * jax.random.normal(next(keys), shape, F32)

    def a_log(shape):
        return jnp.log(jax.random.uniform(next(keys), shape, F32, 1.0, 16.0))

    def dt_bias(shape):
        dt = jnp.exp(jax.random.uniform(next(keys), shape, F32, math.log(1e-3), math.log(1e-1)))
        return dt + jnp.log(-jnp.expm1(-dt))

    L, D = DEPTH, D_MODEL
    return {
        'x': normal((BATCH, SEQ, D), 1.0),
        'c': normal((BATCH, D), 1.0),
        'ctx': normal((BATCH, CTX_LEN, D), 1.0),
        'c_ctx': normal((D,), 1.0),
        'w_ada': normal((L, D, 6 * D), D ** -0.5),
        'b_ada': normal((L, 6 * D), 0.02),
        'norm1_g': gain((L, D)),
        'norm2_g': gain((L, D)),
        'w_in': normal((L, D, D_IN), D ** -0.5),
        'na_q_gain': gain((L, NA_DIM)),
        'na_k_gain': gain((L, NA_DIM)),
        'na_rpb': normal((L, NA_HEADS, 2 * WIN_R - 1, 2 * WIN_C - 1), 0.1),
        'dn_conv_w': normal((L, CONV_W, 2 * DN_KW + DN_VW), CONV_W ** -0.5),
        'dn_a_log': a_log((L, 2, DN_HEADS)),
        'dn_dt_bias': dt_bias((L, 2, DN_HEADS)),
        'dn_o_gain': gain((L, DN_DV)),
        'ssd_conv_w': normal((L, CONV_W, SSD_XBC), CONV_W ** -0.5),
        'ssd_conv_b': normal((L, SSD_XBC), 0.02),
        'ssd_a_log': a_log((L, 2, SSD_HEADS)),
        'ssd_dt_bias': dt_bias((L, 2, SSD_HEADS)),
        'ssd_d': gain((L, SSD_HEADS)),
        'ssd_o_gain': gain((L, SSD_DI)),
        'w_pa': normal((L, NA_W, D), NA_W ** -0.5),
        'w_pb': normal((L, DN_VW, D), DN_VW ** -0.5),
        'w_pc': normal((L, SSD_DI, D), SSD_DI ** -0.5),
        'w_out': normal((L, D, D), D ** -0.5),
        'w_ff1': normal((L, D, D_FF), D ** -0.5),
        'w_ff2': normal((L, D_FF, D), D_FF ** -0.5),
    }

def reference(x, c, ctx, c_ctx, w_ada, b_ada, norm1_g, norm2_g, w_in, na_q_gain, na_k_gain, na_rpb,
              dn_conv_w, dn_a_log, dn_dt_bias, dn_o_gain, ssd_conv_w, ssd_conv_b, ssd_a_log,
              ssd_dt_bias, ssd_d, ssd_o_gain, w_pa, w_pb, w_pc, w_out, w_ff1, w_ff2):
    xc = ctx
    for l in range(DEPTH):
        need_ctx = l < DEPTH - 1
        mod = jnp.split((jax.nn.silu(c) @ w_ada[l] + b_ada[l])[:, None, :], 6, axis=-1)
        mod_c = jnp.split(jax.nn.silu(c_ctx) @ w_ada[l] + b_ada[l], 6, axis=-1)
        h = modulate(rms_norm(x, norm1_g[l]), mod[0], mod[1])
        hc = modulate(rms_norm(xc, norm1_g[l]), mod_c[0], mod_c[1])
        y, yc = token_mixer(h, hc, w_in[l], na_q_gain[l], na_k_gain[l], na_rpb[l],
                            dn_conv_w[l], dn_a_log[l], dn_dt_bias[l], dn_o_gain[l],
                            ssd_conv_w[l], ssd_conv_b[l], ssd_a_log[l], ssd_dt_bias[l], ssd_d[l], ssd_o_gain[l],
                            w_pa[l], w_pb[l], w_pc[l], w_out[l], need_ctx)
        x = x + mod[2] * y
        x = x + mod[5] * squared_relu_mlp(modulate(rms_norm(x, norm2_g[l]), mod[3], mod[4]), w_ff1[l], w_ff2[l])
        if need_ctx:
            xc = xc + mod_c[2] * yc
            xc = xc + mod_c[5] * squared_relu_mlp(
                modulate(rms_norm(xc, norm2_g[l]), mod_c[3], mod_c[4]), w_ff1[l], w_ff2[l])
    return x


_drawn_inputs = setup_inputs


def setup_inputs(seed=0):
    import zlib

    import numpy as np

    out = dict(_drawn_inputs(seed))
    spreads = {}
    factors = {'norm1_g': 3.722,
     'norm2_g': 2.726,
     'na_q_gain': 8.0,
     'na_k_gain': 8.0,
     'na_rpb': 26.896,
     'dn_o_gain': 8.0,
     'ssd_conv_b': 20.001,
     'ssd_d': 64.0,
     'ssd_o_gain': 35.525}
    for name, (base, spread) in spreads.items():
        noise = np.random.default_rng([zlib.crc32(name.encode()), seed]).standard_normal(out[name].shape)
        drawn = base * np.exp(spread * noise) if base else spread * noise
        out[name] = jnp.asarray(drawn.astype(out[name].dtype))
    for name, factor in factors.items():
        out[name] = (out[name] * factor).astype(out[name].dtype)
    return out
```

```python
import math

import numpy as np
import concourse.bass as bass
from concourse import mybir

F32 = mybir.dt.float32
ACT = mybir.ActivationFunctionType
ALU = mybir.AluOpType
AX = mybir.AxisListType

P = 128
D = 1024
KC = D // P
CTX, LAT = 256, 512
T = CTX + LAT
NT = T // P
DEPTH = 2
GW = 64
GR = LAT // GW
HD = 64
NAH, DNH, SSH = 8, 8, 16
WIN_C = 16
BLK_C = 16
BIAS_W = 48
FF = 4 * D
EPS = 1e-6
NEG = -1.0e30
SEGS = ((CTX, LAT), (0, CTX))
RAWW = T + 6
RAW0 = (2, CTX + 4)

RING = 4
PANEL = 2048

ADA_P, GRP_P = 6 * D // 256, 3
PANELS = dict(ada=ADA_P, na0=3, na1=3, dn0=4, dn1=4, ss0=5, ss1=5, merge=20, out=4, ff1=FF // 256, ff2=2 * KC)
JOBS = dict(na0=6, na1=6, dn0=8, dn1=8, ss0=10, ss1=10, merge=48, out=KC, ff1=FF // P, ff2=KC)


def offsets(counts):
    at, out = 0, {}
    for name, n in counts.items():
        out[name] = at
        at += n
    return out, at


PANEL_AT, NPANEL = offsets(PANELS)
JOB_AT, NJOB = offsets(JOBS)

COLS = dict(b_ada=48, n1=8, n2=8, dncv=60, sscv=60, sscb=12, qg=1, kg=1, dng=1, ssd=8, ssg=8)
COL_AT, NCOL = offsets(COLS)
NSM = 64
NDEC = 48


def dec_col(kind, d, h):
    return 24 * d + (h if kind == "dn" else 8 + h)


def level_masks():
    p = np.arange(P)[:, None]
    f = np.arange(P)[None, :]
    out = []
    for l in range(7):
        s = 1 << l
        out.append(((p // (2 * s) == f // (2 * s)) & (p // s % 2 == 1) & (f // s % 2 == 0)).astype(np.float32))
    return out


def constants():
    p = np.arange(P)[:, None]
    f = np.arange(P)[None, :]
    sq = [p == f, np.ones((P, P), bool), p // 64 == f // 64, p <= f, p >= f, p < f, p > f]
    sq = [a.astype(np.float32) for a in sq]
    rot = np.zeros((P, P), np.float32)
    for o in range(P):
        if o % 32 < 16:
            rot[o + 16, o] = -1.0
        else:
            rot[o - 16, o] = 1.0
    lm = level_masks()
    sq += [rot] + lm + [a.T for a in lm]
    square = np.concatenate(sq, axis=1)
    tok = np.arange(LAT)
    quarter = 16
    inv = (10000.0 ** (-np.arange(quarter, dtype=np.float32) / np.float32(quarter))).astype(np.float32)
    d = np.arange(P) % 64
    pos = np.where(d[:, None] < 32, tok[None, :] // GW, tok[None, :] % GW).astype(np.float32)
    ang = (pos * inv[d % 16][:, None]).astype(np.float32)
    trig = np.concatenate([np.cos(ang), np.sin(ang)], axis=1).astype(np.float32)
    nam = np.zeros((GR, BLK_C, 3, GR, 32), np.float32)
    for v, b in enumerate((0, 1, 3)):
        start = min(max(b * BLK_C - 8, 0), GW - 32)
        for i in range(BLK_C):
            w = min(max(b * BLK_C + i - WIN_C // 2, 0), GW - WIN_C) - start
            ok = np.zeros(32, bool)
            ok[w:w + WIN_C] = True
            nam[:, i, v] = np.where(ok, 0.0, NEG)
    return np.ascontiguousarray(np.concatenate([square, trig, nam.reshape(P, -1)], axis=1), dtype=np.float32)


SQ = ["ident", "ones", "bones", "le", "ge", "lt", "gt", "rot"] + [f"lm{i}" for i in range(7)] + [f"um{i}" for i in range(7)]
NCONST = len(SQ) * P + 2 * LAT + 3 * 256


class Steps:

    def __init__(self, sem, names):
        self.sem, self.names = sem, list(names)

    def at(self, step, name):
        return step * len(self.names) + self.names.index(name) + 1


def build(nc, x_in, c_in, stream, wsmall_in, cols_in, rows_in, rpb_in, const_in, out):
    def sb(name, n):
        return nc.alloc_sbuf_tensor(name, [P, n], F32)

    X = sb("X", KC * T)[:, :].rearrange("p (k t) -> p k t", k=KC)
    H = sb("H", KC * T)[:, :].rearrange("p (k t) -> p k t", k=KC)
    ring = sb("ring", RING * PANEL)
    cst = sb("cst", NCONST)
    C = {n: cst[:, i * P:(i + 1) * P] for i, n in enumerate(SQ)}
    cos = cst[:, len(SQ) * P:len(SQ) * P + LAT]
    sin = cst[:, len(SQ) * P + LAT:len(SQ) * P + 2 * LAT]
    nam = cst[:, len(SQ) * P + 2 * LAT:].rearrange("p (v x) -> p v x", v=3)
    prm = sb("prm", NCOL)
    rowp = sb("rowp", 2 * NDEC)
    cvec = sb("cvec", 2 * KC)[:, :].rearrange("p (k s) -> p k s", s=2)
    scv = sb("scv", 2 * KC)[:, :].rearrange("p (k s) -> p k s", s=2)
    mod = sb("mod", 96)[:, :].rearrange("p (f s) -> p f s", s=2)
    am = sb("am", 16)[:, :].rearrange("p (f s) -> p f s", s=2)
    qg8 = sb("qg8", 1)
    wsm = sb("wsm", KC * NSM)[:, :].rearrange("p (k c) -> p k c", k=KC)
    beta = sb("beta", NT * 16)[:, :].rearrange("p (t c) -> p t c", t=NT)
    spl = sb("spl", NT * NDEC)[:, :].rearrange("p (t c) -> p t c", t=NT)
    dec = sb("dec", NT * NDEC)[:, :].rearrange("p (t c) -> p t c", t=NT)
    EXX = sb("EXX", 3 * NT * NDEC)[:, :].rearrange("p (t e c) -> p t e c", t=NT, e=3)
    smt = sb("smt", 24)
    eps_t, extra_t = sb("eps_t", 1), sb("extra_t", 1)
    arena_n = 25400
    ar = sb("arena", arena_n)
    top = [0]

    def take(n):
        a = ar[:, top[0]:top[0] + n]
        top[0] += n
        assert top[0] <= arena_n, top[0]
        return a

    YA = take(4 * T).rearrange("p (k t) -> p k t", k=4)
    YB = take(4 * T).rearrange("p (k t) -> p k t", k=4)
    mixer0 = top[0]

    naq = take(4 * T).rearrange("p (k t) -> p k t", k=4)
    nav = take(2 * T).rearrange("p (k t) -> p k t", k=2)
    nasq = take(2 * T).rearrange("p (k t) -> p k t", k=2)
    nars = take(2 * T).rearrange("p (k t) -> p k t", k=2)
    navt = take(10 * 256).rearrange("p (t c) -> p t c", t=10)
    nag = take(4 * GR * BIAS_W).rearrange("p (h r m) -> p h r m", h=4, r=GR)
    nab = take(4 * 3 * 256).rearrange("p (h v x) -> p h v x", h=4, v=3)
    naP = take(2 * 512).rearrange("p (b x) -> p b x", b=2)
    naPT = take(2 * 512).rearrange("p (b x) -> p b x", b=2)
    naO = take(2 * 256).rearrange("p (b x) -> p b x", b=2)
    nast = take(3 * 64).rearrange("p (s x) -> p s x", s=3)
    rpbp = take(64)

    top[0] = mixer0
    QK = take(4 * T).rearrange("p (k t) -> p k t", k=4)
    kvt = take(NT * 512).rearrange("p (t c) -> p t c", t=NT)
    zb = take(2 * T).rearrange("p (k t) -> p k t", k=2)
    dno = take(NT * 256).rearrange("p (t c) -> p t c", t=NT)
    dnS = take(2 * 256).rearrange("p (d g v) -> p d g v", d=2, g=2)
    after_o = top[0]
    dnV = take(2 * T).rearrange("p (k t) -> p k t", k=2)
    rawp = take(2 * RAWW).rearrange("p (b t) -> p b t", b=2)
    cv = take(2 * RAWW).rearrange("p (b t) -> p b t", b=2)
    sqb = take(2 * T).rearrange("p (b t) -> p b t", b=2)
    rsb = take(2 * T).rearrange("p (b t) -> p b t", b=2)
    top[0] = after_o

    def per_dir(n, h=4):
        return [take(n).rearrange("p (h x) -> p h x", h=h) for _ in range(2)]

    dR, dD = per_dir(512), per_dir(512)
    dDM, dMT, dX, dXT = per_dir(512), per_dir(512), per_dir(512), per_dir(512)
    dAT = per_dir(512)
    dY = dR
    dKE, dKD, dVN = per_dir(256), per_dir(256), per_dir(256)
    dTmp = [x[:, 0:2].rearrange("p a (b x) -> p (a b) x", b=2) for x in dX]
    dWT = per_dir(256, 2)
    dDA = dD

    top[0] = mixer0
    YC = take(8 * T).rearrange("p (k t) -> p k t", k=8)
    BC = take(2 * T).rearrange("p (k t) -> p k t", k=2)
    xt = take(NT * 512).rearrange("p (t c) -> p t c", t=NT)
    bt = take(NT * P).rearrange("p (t c) -> p t c", t=NT)
    yt = take(NT * 512).rearrange("p (t c) -> p t c", t=NT)
    ssH = take(2 * 512).rearrange("p (d x) -> p d x", d=2)
    after_h = top[0]
    srawp = take(2 * RAWW).rearrange("p (b t) -> p b t", b=2)
    scvb = take(2 * RAWW).rearrange("p (b t) -> p b t", b=2)
    top[0] = after_h
    sR = [take(512) for _ in range(2)]
    sCB = [take(128) for _ in range(2)]
    sXD = [take(512) for _ in range(2)]
    sW = [take(512) for _ in range(2)]
    szb = xt.rearrange("p t c -> p (t c)").rearrange("p (k t) -> p k t", k=4)
    ssq = yt.rearrange("p t c -> p (t c)").rearrange("p (k t) -> p k t", k=4)
    srs = bt.rearrange("p t c -> p (t c)")
    top[0] = mixer0 + 8 * T
    gates = take(6 * T).rearrange("p (k t) -> p k t", k=6)
    mt = take(8 * T).rearrange("p (k t) -> p k t", k=8)
    mtmp = take(T)
    top[0] = 0
    nsq = take(2 * T).rearrange("p (b t) -> p b t", b=2)
    nrs = take(T)
    top[0] = 0
    hid = take(FF // P * T).rearrange("p (k t) -> p k t", k=FF // P)

    ps = [nc.alloc_psum_tensor(f"ps{i}", [P, 512], F32)[:, :] for i in range(8)]

    na_obank, na_tbank = (ps[7], ps[3]), (ps[2], ps[0])

    dn_scr = ar[:, after_o:after_o + NT * 256]

    def sem(name):
        return nc.alloc_semaphore(name)

    slot_full = [sem(f"slot_full{i}") for i in range(RING)]
    x_in_s, cst_in, c_in_s, prm_in, row_in, wsm_in, rpb_ld = (sem(n) for n in ("x_in_s", "cst_in", "c_in_s", "prm_in", "row_in", "wsm_in", "rpb_ld"))
    dense_done = sem("dense_done")
    dense_free = [sem("dense_free0"), sem("dense_free1")]
    ada_done, mod_ready, scv_ready = sem("ada_done"), sem("mod_ready"), sem("scv_ready")
    sq_ready, nsum_ready, nrs_ready, h_ready, x_ready = (sem(n) for n in ("sq_ready", "nsum_ready", "nrs_ready", "h_ready", "x_ready"))
    sm_done, cum_done, exx_ready, decay_ready = (sem(n) for n in ("sm_done", "cum_done", "exx_ready", "decay_ready"))
    sm_act, sm_dve = sem("sm_act"), sem("sm_dve")
    na_sq, na_ss, na_rs, na_qk, na_vt, na_vc, na_bias = (sem(n) for n in ("na_sq", "na_ss", "na_rs", "na_qk", "na_vt", "na_vc", "na_bias"))
    na_S, na_max, na_P, na_T, na_PT, na_PV, na_O, na_OT, na_YA = (sem(n) for n in ("na_S", "na_max", "na_P", "na_T", "na_PT", "na_PV", "na_O", "na_OT", "na_YA"))
    conv_done, silu_done, pads_ready = sem("conv_done"), sem("silu_done"), sem("pads_ready")
    dq_sq, dq_ss, dq_rs, dq_n, dq_rot, dq_rope = (sem(n) for n in ("dq_sq", "dq_ss", "dq_rs", "dq_n", "dq_rot", "dq_rope"))
    tr_done, tr_copied = sem("tr_done"), sem("tr_copied")
    dn_ss, dn_rs, dn_on, dn_ot, dn_y = (sem(n) for n in ("dn_ss", "dn_rs", "dn_on", "dn_ot", "dn_y"))
    ss_ot, ss_yz, ss_sq, ss_sum, ss_rs, ss_y = (sem(n) for n in ("ss_ot", "ss_yz", "ss_sq", "ss_sum", "ss_rs", "ss_y"))
    hid_relu, hid_ready, m_ready, out_done = sem("hid_relu"), sem("hid_ready"), sem("m_ready"), sem("out_done")
    eps_ready = sem("eps_ready")
    act_chain, dve_chain, pool_chain = sem("act_chain"), sem("dve_chain"), sem("pool_chain")

    LV = range(1, 7)
    pe_n = ["SEG", "GK", "GQ", "T0"]
    dve_n = ["MT", "AT", "XT1"]
    act_n = ["D", "X1"]
    for l in LV:
        pe_n += [f"Y{l}", f"Z{l}"] + ([f"T{l}"] if l < 6 else [])
        dve_n += [f"Y{l}", f"X{l}"]
        if l < 6:
            act_n += [f"XT{l}"]
    pe_n += ["WT", "V", "OI", "OA", "ST"]
    dve_n += ["VN", "O", "S"]
    act_n += ["WT"]
    dpe = [Steps(sem(f"dn_pe{d}"), pe_n) for d in range(2)]
    ddve = [Steps(sem(f"dn_dve{d}"), dve_n) for d in range(2)]
    dact = [Steps(sem(f"dn_act{d}"), act_n) for d in range(2)]
    dpool = [Steps(sem(f"dn_pool{d}"), ["R", "KE", "KD", "DM", "DA"]) for d in range(2)]
    spe = [Steps(sem(f"ss_pe{d}"), ["SEG0", "CB", "SEG1", "Y0", "Y1", "INT", "ST"]) for d in range(2)]
    sdve = [Steps(sem(f"ss_dve{d}"), ["CBM", "XD", "W0", "W1", "YA", "H"]) for d in range(2)]
    sact = [Steps(sem(f"ss_act{d}"), ["D0", "D1"]) for d in range(2)]
    spool = [Steps(sem(f"ss_pool{d}"), ["R0", "R1", "XW"]) for d in range(2)]

    TILES = ((0, 1, 2, 3, 4, 5), (1, 0, 5, 4, 3, 2))

    def first_visit(n):
        return n in (0, 2, 3)

    def job(layer, stage, i):
        return layer * NJOB + JOB_AT[stage] + i

    def segs_of(layer):
        return SEGS if layer < DEPTH - 1 else SEGS[:1]

    def na_blocks(layer):
        return ([(False, 0), (False, 1)] if layer < DEPTH - 1 else []) + [(True, b) for b in range(4)]

    def flat(a):
        return a.rearrange("p a b -> p (a b)")

    def na_u0(layer, gi):
        return sum(2 * 4 * len(na_blocks(l)) for l in range(layer)) + gi * 4 * len(na_blocks(layer))

    def counted(j):
        r = j % NJOB
        return not (JOB_AT["out"] <= r < JOB_AT["ff1"] or r >= JOB_AT["ff2"])

    def free_count(j):
        return sum(counted(i) for i in range(j % 2, j + 1, 2))

    def bcast(a, n):
        return a.unsqueeze(2).to_broadcast([a.shape[0], a.shape[1], n])

    def over(a, h):
        return a.unsqueeze(1).to_broadcast([a.shape[0], h, a.shape[1]])

    def col(layer, name, i=0):
        at = COL_AT[name] + i
        return prm[:, at:at + 1]

    def window(b):
        return min(max(b * BLK_C - 8, 0), GW - 32)

    def nak(a, b):
        return a.rearrange("p (r c) -> p c r", r=GR)[:, window(b):window(b) + 32]

    def by_block(a):
        return a.rearrange("p (b r i) -> p r b i", b=4, r=GR)

    def by_column(a):
        return a.rearrange("p (c r) -> p r c", r=GR)

    def naq_of(a, b):
        return a.rearrange("p (r c) -> p r c", r=GR)[:, :, b * BLK_C:(b + 1) * BLK_C]

    VAR = (0, 1, 1, 2)

    block_ctx = nc.Block()
    with block_ctx as block:

        @block.sync
        def _(sp):
            def released():
                out = []
                for layer in range(DEPTH):
                    base = layer * NJOB
                    out += [(ada_done, layer * ADA_P + i + 1) for i in range(ADA_P)]
                    for st in ("na0", "na1", "dn0", "dn1", "ss0", "ss1"):
                        out += [(dense_done, base + JOB_AT[st] + 2 * i + 2) for i in range(PANELS[st])]
                    for m in range(4):
                        out += [(dense_done, base + JOB_AT["merge"] + 12 * m + e) for e in (2, 4, 6, 10, 12)]
                    out += [(dense_done, base + JOB_AT["out"] + 2 * i + 2) for i in range(4)]
                    out += [(dense_done, base + JOB_AT["ff1"] + 2 * i + 2) for i in range(FF // 256)]
                    out += [(dense_done, base + JOB_AT["ff2"] + i // 2 + 1) for i in range(2 * KC)]
                return out

            uses = released()
            for n in range(DEPTH * NPANEL):
                if n >= RING:
                    s, v = uses[n - RING]
                    sp.wait_ge(s, v)
                sp.dma_start(ring[:, n % RING * PANEL:(n % RING + 1) * PANEL], stream[n]).then_inc(slot_full[n % RING], 16)
                if n == 0:
                    sp.dma_start(cst[:, :], const_in).then_inc(cst_in, 16)
            for k in range(KC):
                sp.wait_ge(x_ready, 2 * KC * DEPTH - KC + k + 1)
                sp.dma_start(out[:, k, :], X[:, k, CTX:]).then_inc(out_done, 16)
            sp.wait_ge(out_done, 16 * KC)

        @block.gpsimd
        def _(pool):
            chain = [0]

            def link(ins):
                chain[0] += 1
                ins.then_inc(pool_chain, 1)
                pool.wait_ge(pool_chain, chain[0])

            g = nc.gpsimd
            g.dma_start(cvec, c_in).then_inc(c_in_s, 16)
            g.dma_start(X[:, :, :], x_in).then_inc(x_in_s, 16)
            for layer in range(DEPTH):
                if layer:
                    pool.wait_ge(h_ready, 2 * layer)
                g.dma_start(prm[:, :], cols_in[layer]).then_inc(prm_in, 16)
                g.dma_start(rowp[:, :], rows_in[layer].partition_broadcast(P)).then_inc(row_in, 16)
                g.dma_start(wsm, wsmall_in[layer]).then_inc(wsm_in, 16)
                for gi in range(2):
                    G = 2 * layer + gi
                    pool.wait_ge(h_ready, 2 * layer + 1)
                    if gi:
                        pool.wait_ge(na_bias, G)
                    for r in range(GR):
                        src = rpb_in[layer, 4 * gi:4 * gi + 4, :, GR - 1 - r:2 * GR - 1 - r, :]
                        g.dma_start(nag[r * BLK_C:(r + 1) * BLK_C], src.rearrange("h i r m -> i h r m")).then_inc(rpb_ld, 16)
                    pool.wait_ge(rpb_ld, 16 * GR * (G + 1))
                    if gi == 1:
                        pool.wait_ge(na_max, na_u0(layer, 1))
                    for h in range(4):
                        for v, m0 in enumerate((16, 8, 0)):
                            ins = g.tensor_tensor(nab[:, h, v].rearrange("p (c r) -> p r c", r=GR), nag[:, h, :, m0:m0 + 32],
                                                  nam[:, v].rearrange("p (r c) -> p r c", r=GR), ALU.add)
                    ins.then_inc(na_bias, 1)
                for hg in range(2):
                    G = 2 * layer + hg
                    pool.wait_ge(tr_copied, 6 * (4 * layer + hg + 1))
                    for n in range(6):
                        s = 6 * G + n
                        for d in range(2):
                            t = TILES[d][n]
                            c0 = dec_col("dn", d, 4 * hg)
                            inc_m, dec_g = (C["le"], C["ge"])[d], dec[:, t, c0:c0 + 4]
                            if s:
                                pool.wait_ge(dpe[d].sem, dpe[d].at(s - 1, "Z6"))
                            g.tensor_tensor(dR[d], over(inc_m, 4), bcast(dec_g, P), ALU.mult).then_inc(dpool[d].sem, 1)
                            if s:
                                pool.wait_ge(dpe[d].sem, dpe[d].at(s - 1, "ST"))
                            kk = kvt[:, t, 0:256].rearrange("p (h x) -> p h x", h=4)
                            g.tensor_tensor(dKE[d], kk, bcast(EXX[:, t, 0, c0:c0 + 4], 64), ALU.mult).then_inc(dpool[d].sem, 1)
                            g.tensor_tensor(dKD[d], kk, bcast(EXX[:, t, 1, c0:c0 + 4], 64), ALU.mult).then_inc(dpool[d].sem, 1)
                        for d in range(2):
                            t = TILES[d][n]
                            strict = (C["lt"], C["gt"])[d]
                            pool.wait_ge(dact[d].sem, dact[d].at(s, "D"))
                            link(g.tensor_tensor(dDM[d], dD[d], over(strict, 4), ALU.mult))
                            g.tensor_tensor(dDM[d], dDM[d], bcast(beta[:, t, 8 * d + 4 * hg:8 * d + 4 * hg + 4], P), ALU.mult).then_inc(dpool[d].sem, 1)
                            g.tensor_tensor(dDA[d], dD[d], over((C["le"], C["ge"])[d], 4), ALU.mult).then_inc(dpool[d].sem, 1)
                for sg in range(2):
                    G = 2 * layer + sg
                    pool.wait_ge(tr_copied, 6 * (4 * layer + 2 + sg + 1))
                    for n in range(6):
                        s = 6 * G + n
                        for d in range(2):
                            t = TILES[d][n]
                            if s:
                                pool.wait_ge(spe[d].sem, spe[d].at(s - 1, "ST"))
                            for half in range(2):
                                if half:
                                    pool.wait_ge(spe[d].sem, spe[d].at(s, "SEG0"))
                                c0 = dec_col("ss", d, 8 * sg + 4 * half)
                                g.tensor_tensor(sR[d].rearrange("p (h x) -> p h x", h=4), over((C["le"], C["ge"])[d], 4),
                                                bcast(dec[:, t, c0:c0 + 4], P), ALU.mult).then_inc(spool[d].sem, 1)
                        for d in range(2):
                            t = TILES[d][n]
                            c0 = dec_col("ss", d, 8 * sg)
                            pool.wait_ge(spe[d].sem, spe[d].at(s, "SEG1"))
                            pool.wait_ge(sdve[d].sem, sdve[d].at(s, "XD"))
                            g.tensor_tensor(sR[d].rearrange("p (h x) -> p h x", h=8), sXD[d].rearrange("p (h x) -> p h x", h=8),
                                            bcast(EXX[:, t, 1, c0:c0 + 8], 64), ALU.mult).then_inc(spool[d].sem, 1)

        @block.scalar
        def _(act):
            chain = [0]
            a = nc.scalar

            def link(ins):
                chain[0] += 1
                ins.then_inc(act_chain, 1)
                act.wait_ge(act_chain, chain[0])

            def rsqrt(out_ap, in_aps, out_parts, scale, last_sem, extra=0.0):
                for o, i in zip(out_parts, in_aps):
                    ins = a.activation(o, i, ACT.Ln, scale=scale, bias=eps_t[:, 0:1])
                link(ins)
                a.activation(out_ap, out_ap, ACT.Exp, scale=-0.5, bias=(extra_t[:, 0:1] if extra else 0.0)).then_inc(last_sem, 1)

            def norm(q, segs):
                layer = q // 2
                if q == 0:
                    act.wait_ge(x_in_s, 16)
                for k in range(KC):
                    if q:
                        act.wait_ge(x_ready, KC * (q - 1) + k + 1)
                    if q and k == 0:
                        act.wait_ge(x_ready, KC * q)
                    if k >= 2:
                        act.wait_ge(nsum_ready, KC * q + k - 1)
                    lo, hi = (0, T) if len(segs) == 2 else (CTX, T)
                    a.activation(nsq[:, k % 2, lo:hi], X[:, k, lo:hi], ACT.Square).then_inc(sq_ready, 1)
                act.wait_ge(nsum_ready, KC * (q + 1))
                rsqrt(nrs[:, lo:hi], [ps[i][:, 0:w] for i, (o, w) in enumerate(segs)], [nrs[:, o:o + w] for o, w in segs],
                      1.0 / D, nrs_ready)

            def evac(j, outs, func=ACT.Copy, segs=SEGS):
                act.wait_ge(dense_done, j + 1)
                for i, (o, w) in enumerate(segs):
                    ins = a.activation(outs[i], ps[2 * (j % 2) + i][:, 0:w], func)
                return ins

            def group_proj(layer, stage, gq, raw_b, cv_b, dests, zj, z_dest, bias_cols):
                act.wait_ge(pads_ready, gq + 1)
                for c in range(7):
                    if c < 6:
                        if c >= 2:
                            act.wait_ge(conv_done, 6 * gq + c - 1)
                        j = job(layer, stage, c)
                        evac(j, [raw_b[:, c % 2, RAW0[1]:RAW0[1] + LAT], raw_b[:, c % 2, 2:2 + CTX]]).then_inc(dense_free[j % 2], 1)
                    if c >= 1:
                        act.wait_ge(conv_done, 6 * gq + c)
                        for o, w, r0 in ((CTX, LAT, RAW0[1]), (0, CTX, 2)):
                            b = prm[:, bias_cols + c - 1:bias_cols + c] if bias_cols is not None else 0.0
                            ins = a.activation(dests[c - 1][:, o:o + w], cv_b[:, (c - 1) % 2, r0:r0 + w], ACT.Silu, bias=b)
                        ins.then_inc(silu_done, 1)
                for c in range(zj):
                    j = job(layer, stage, 6 + c)
                    evac(j, [z_dest[:, c, o:o + w] for o, w in SEGS], ACT.Silu).then_inc(dense_free[j % 2], 1)

            act.wait_ge(c_in_s, 16)
            act.wait_ge(eps_ready, 2)
            a.activation(scv, cvec, ACT.Silu).then_inc(scv_ready, 1)
            for layer in range(DEPTH):
                segs = segs_of(layer)
                norm(2 * layer, SEGS)
                act.wait_ge(row_in, 16 * (layer + 1))
                link(a.activation(rowp[:, NDEC:], rowp[:, NDEC:], ACT.Exp))
                act.wait_ge(sm_done, layer + 1)
                smp = ps[6][:, 0:NT * NSM].rearrange("p (t c) -> p t c", t=NT)
                a.activation(beta, smp[:, :, 0:16], ACT.Exp, scale=-1.0).then_inc(sm_act, 1)
                act.wait_ge(sm_dve, 2 * layer + 1)
                link(a.activation(spl, dec, ACT.Abs))
                link(a.activation(spl, spl, ACT.Exp, scale=-1.0))
                a.activation(spl, spl, ACT.Ln, bias=1.0).then_inc(sm_act, 1)
                act.wait_ge(cum_done, layer + 1)
                for i in range(2):
                    ins = a.activation(EXX[:, 3 * i:3 * i + 3].rearrange("p t e c -> p (t e c)"), ps[4 + i][:, 0:9 * NDEC], ACT.Exp)
                ins.then_inc(exx_ready, 1)
                blocks = na_blocks(layer)
                units = [(b, h) for b in range(len(blocks)) for h in range(4)]
                for gi in range(2):
                    G = 2 * layer + gi
                    for c in range(6):
                        j = job(layer, f"na{gi}", c)
                        dst = naq[:, c] if c < 4 else nav[:, c - 4]
                        act.wait_ge(dense_done, j + 1)
                        lat = ps[2 * (j % 2)]
                        if c < 2:
                            a.activation(by_block(dst[:, CTX:]), lat.rearrange("p (r b i) -> p r b i", b=4, r=GR), ACT.Copy)
                        elif c < 4:
                            a.activation(dst[:, CTX:], lat, ACT.Copy)
                        else:
                            a.activation(by_column(dst[:, CTX:]), lat.rearrange("p (r c) -> p r c", r=GR), ACT.Copy)
                        a.activation(dst[:, 0:CTX], ps[2 * (j % 2) + 1][:, 0:CTX], ACT.Copy).then_inc(dense_free[j % 2], 1)
                        if c < 4:
                            if c >= 2:
                                act.wait_ge(na_ss, 4 * G + c - 1)
                            act.wait_ge(dense_free[j % 2], free_count(j))
                            a.activation(nasq[:, c % 2], dst, ACT.Square).then_inc(na_sq, 1)
                        if 1 <= c <= 4:
                            cc = c - 1
                            act.wait_ge(na_ss, 4 * G + cc + 1)
                            if cc >= 2:
                                act.wait_ge(na_qk, 4 * G + cc - 1)
                            rsqrt(nars[:, cc % 2], [ps[4 + 2 * (cc % 2) + i][:, 0:w] for i, (o, w) in enumerate(SEGS)],
                                  [nars[:, cc % 2, o:o + w] for o, w in SEGS], 1.0 / HD, na_rs)
                    for i in range(5):
                        act.wait_ge(na_vt, 5 * G + i + 1)
                        a.activation(navt[:, 2 * i:2 * i + 2].rearrange("p t c -> p (t c)"), ps[4 + i % 4], ACT.Copy).then_inc(na_vc, 1)
                    u0 = na_u0(layer, gi)
                    b0 = u0 // 4

                    def probs(u):
                        lat = blocks[units[u][0]][0]
                        act.wait_ge(na_max, u0 + u + 1)
                        lo = 0 if lat else 256
                        if u >= 2:
                            act.wait_ge(na_T, u0 + u - 1)
                        hcol = units[u][0] % 2 * 4 + units[u][1]
                        a.activation(naP[:, u % 2, lo:512], ps[4 + u % 2][:, lo:512], ACT.Exp, bias=nast[:, 0, u % 2:u % 2 + 1],
                                     accum_out=nast[:, 1, hcol:hcol + 1]).then_inc(na_P, 1)

                    def ya(b):
                        lat, i = blocks[b]
                        act.wait_ge(na_OT, b0 + b + 1)
                        for c in range(2):
                            src = na_tbank[b % 2][:, c * P:(c + 1) * P]
                            if lat:
                                dst = naq_of(YA[:, 2 * gi + c, CTX:], i)
                                ins = a.activation(dst, src.rearrange("p (r c) -> p r c", r=GR), ACT.Copy)
                            else:
                                ins = a.activation(YA[:, 2 * gi + c, i * P:(i + 1) * P], src, ACT.Copy)
                        ins.then_inc(na_YA, 1)

                    probs(0)
                    for u in range(len(units)):
                        if u + 1 < len(units):
                            probs(u + 1)
                        lo = 0 if blocks[units[u][0]][0] else 256
                        act.wait_ge(na_T, u0 + u + 1)
                        if u >= 2:
                            act.wait_ge(na_PV, u0 + u - 1)
                        a.activation(naPT[:, u % 2, lo:512], ps[6][:, lo:512], ACT.Copy).then_inc(na_PT, 1)
                        if units[u][1] == 1 and units[u][0] > 0:
                            ya(units[u][0] - 1)
                    ya(len(blocks) - 1)
                for hg in range(2):
                    G = 2 * layer + hg
                    gq = 4 * layer + hg
                    group_proj(layer, f"dn{hg}", gq, rawp, cv, [QK[:, 0], QK[:, 1], QK[:, 2], QK[:, 3], dnV[:, 0], dnV[:, 1]], 2, zb, None)
                    for c in range(4):
                        act.wait_ge(silu_done, 6 * gq + c + 1)
                        a.activation(sqb[:, c % 2], QK[:, c], ACT.Square).then_inc(dq_sq, 1)
                        act.wait_ge(dq_ss, 4 * G + c + 1)
                        if c >= 2:
                            act.wait_ge(dq_rope, 4 * G + c - 1)
                        rsqrt(rsb[:, c % 2], [ps[4 + 2 * (c % 2) + i][:, 0:w] for i, (o, w) in enumerate(SEGS)],
                              [rsb[:, c % 2, o:o + w] for o, w in SEGS], 1.0, dq_rs, extra=(1.0 if c < 2 else 0.0))
                    for t in range(NT):
                        act.wait_ge(tr_done, 6 * gq + t + 1)
                        a.activation(kvt[:, t], ps[4 + t % 4], ACT.Copy).then_inc(tr_copied, 1)
                    for n in range(6):
                        s = 6 * G + n
                        for d in range(2):
                            act.wait_ge(dpe[d].sem, dpe[d].at(s, "SEG"))
                            if s:
                                act.wait_ge(ddve[d].sem, ddve[d].at(s - 1, "AT"))
                            a.activation(flat(dD[d]), ps[4 * d], ACT.Exp).then_inc(dact[d].sem, 1)
                        for d in range(2):
                            act.wait_ge(dpe[d].sem, dpe[d].at(s, "T0"))
                            a.activation(flat(dX[d]), ps[4 * d + 2], ACT.Copy).then_inc(dact[d].sem, 1)
                        for l in range(1, 6):
                            for d in range(2):
                                act.wait_ge(dpe[d].sem, dpe[d].at(s, f"T{l}"))
                                a.activation(flat(dXT[d]), ps[4 * d + 2], ACT.Copy).then_inc(dact[d].sem, 1)
                        for d in range(2):
                            act.wait_ge(dpe[d].sem, dpe[d].at(s, "WT"))
                            a.activation(flat(dWT[d]), ps[4 * d][:, 0:256], ACT.Copy, scale=-1.0).then_inc(dact[d].sem, 1)
                    act.wait_ge(dn_ss, G + 1)
                    rsqrt(smt[:, 0:24], [smt[:, 0:24]], [smt[:, 0:24]], 1.0 / HD, dn_rs)
                for sg in range(2):
                    G = 2 * layer + sg
                    gq = 4 * layer + 2 + sg
                    group_proj(layer, f"ss{sg}", gq, srawp, scvb,
                               [YC[:, 4 * sg + c] for c in range(4)] + [BC[:, 0], BC[:, 1]], 0, None, COL_AT["sscb"] + 6 * sg)
                    for t in range(NT):
                        act.wait_ge(tr_done, 6 * gq + t + 1)
                        a.activation(xt[:, t], ps[4 + t % 2], ACT.Copy)
                        a.activation(bt[:, t], ps[6 + t % 2][:, 0:P], ACT.Copy).then_inc(tr_copied, 1)
                    for n in range(6):
                        s = 6 * G + n
                        for half in range(2):
                            for d in range(2):
                                act.wait_ge(spe[d].sem, spe[d].at(s, f"SEG{half}"))
                                if half:
                                    act.wait_ge(spe[d].sem, spe[d].at(s, "Y0"))
                                elif s:
                                    act.wait_ge(spe[d].sem, spe[d].at(s - 1, "Y1"))
                                a.activation(sW[d], ps[4 * d + half], ACT.Exp).then_inc(sact[d].sem, 1)
                    for d in range(2):
                        act.wait_ge(sdve[d].sem, sdve[d].at(6 * G + 5, "H"))
                    for c in range(4):
                        j = job(layer, f"ss{sg}", 6 + c)
                        evac(j, [szb[:, c, o:o + w] for o, w in SEGS], ACT.Silu).then_inc(dense_free[j % 2], 1)
                    act.wait_ge(ss_yz, NT * (G + 1))
                    act.wait_ge(ss_ot, NT * (G + 1))
                    for c in range(4):
                        a.activation(ssq[:, c], YC[:, 4 * sg + c], ACT.Square).then_inc(ss_sq, 1)
                    act.wait_ge(ss_sum, G + 1)
                    rsqrt(srs, [ps[4 + i][:, 0:w] for i, (o, w) in enumerate(SEGS)], [srs[:, o:o + w] for o, w in SEGS], 1.0 / 512, ss_rs)
                act.wait_ge(ss_y, 2 * (layer + 1))
                for m in range(4):
                    for i in range(6):
                        j = job(layer, "merge", 12 * m + i)
                        if m:
                            act.wait_ge(m_ready, KC * layer + 2 * m)
                        evac(j, [gates[:, i, o:o + w] for o, w in segs], ACT.Sigmoid, segs).then_inc(dense_free[j % 2], 1)
                norm(2 * layer + 1, segs)
                for c in range(FF // P):
                    if c == 0:
                        act.wait_ge(h_ready, 2 * layer + 2)
                    j = job(layer, "ff1", c)
                    evac(j, [hid[:, c, o:o + w] for o, w in segs], ACT.Relu, segs).then_inc(dense_free[j % 2], 1)

        @block.vector
        def _(dve):
            chain = [0]
            v = nc.vector

            def link(ins):
                chain[0] += 1
                ins.then_inc(dve_chain, 1)
                dve.wait_ge(dve_chain, chain[0])

            dve.wait_ge(cst_in, 16)
            v.memset(eps_t[:, :], EPS).then_inc(eps_ready, 1)
            v.memset(extra_t[:, :], -math.log(8.0)).then_inc(eps_ready, 1)

            def modulation(layer):
                if layer:
                    dve.wait_ge(x_ready, 2 * KC * layer)
                dve.wait_ge(ada_done, ADA_P * (layer + 1))
                dve.wait_ge(prm_in, 16 * (layer + 1))
                v.tensor_tensor(mod, ps[7][:, 0:96].rearrange("p (f s) -> p f s", s=2), bcast(prm[:, 0:48], 2), ALU.add).then_inc(mod_ready, 1)
                dve.wait_ge(mod_ready, layer + 1)
                link(v.tensor_scalar(qg8[:, :], col(layer, "qg"), HD ** -0.5, None, ALU.mult))

            def norm(q, segs, part):
                layer = q // 2
                if q:
                    dve.wait_ge(h_ready, q)
                gain = prm[:, COL_AT["n1"] + 8 * part:COL_AT["n1"] + 8 * part + 8]
                link(v.scalar_tensor_tensor(out=am, in0=mod[:, 24 * part + 8:24 * part + 16], scalar=1.0, in1=bcast(gain, 2),
                                            op0=ALU.add, op1=ALU.mult))
                dve.wait_ge(nrs_ready, q + 1)
                lo, hi = (0, T) if len(segs) == 2 else (CTX, T)
                for k in range(KC):
                    link(v.tensor_tensor(H[:, k, lo:hi], X[:, k, lo:hi], nrs[:, lo:hi], ALU.mult))
                    for i, (o, w) in enumerate(segs):
                        ins = v.tensor_scalar(H[:, k, o:o + w], H[:, k, o:o + w], am[:, k, i:i + 1], mod[:, 24 * part + k, i:i + 1], ALU.mult, ALU.add)
                ins.then_inc(h_ready, 1)

            def convs(layer, gq, raw_b, cv_b, taps):
                for b in range(2):
                    ins = v.memset(raw_b[:, b], 0.0)
                ins.then_inc(pads_ready, 1)
                st = "dn" if gq % 4 < 2 else "ss"
                for c in range(6):
                    j = job(layer, f"{st}{gq % 2}", c)
                    dve.wait_ge(dense_free[j % 2], free_count(j))
                    if c >= 2:
                        dve.wait_ge(silu_done, 6 * gq + c - 1)
                    o = cv_b[:, c % 2, 2:RAWW - 2]
                    tap = [prm[:, taps + 5 * c + k:taps + 5 * c + k + 1] for k in range(5)]
                    link(v.tensor_scalar(o, raw_b[:, c % 2, 2:RAWW - 2], tap[2], None, ALU.mult))
                    for k in (0, 1, 3, 4):
                        ins = v.scalar_tensor_tensor(out=o, in0=raw_b[:, c % 2, k:k + T + 2], scalar=tap[k], in1=o, op0=ALU.mult, op1=ALU.add)
                        if k < 4:
                            link(ins)
                    ins.then_inc(conv_done, 1)

            for layer in range(DEPTH):
                segs = segs_of(layer)
                modulation(layer)
                norm(2 * layer, SEGS, 0)
                dve.wait_ge(row_in, 16 * (layer + 1))
                dve.wait_ge(sm_act, 2 * layer + 1)
                smp = ps[6][:, 0:NT * NSM].rearrange("p (t c) -> p t c", t=NT)
                v.tensor_tensor(dec, smp[:, :, 16:NSM], rowp[:, 0:NDEC].unsqueeze(1).to_broadcast([P, NT, NDEC]), ALU.add).then_inc(sm_dve, 1)
                link(v.tensor_scalar(beta, beta, 1.0, None, ALU.add))
                link(v.reciprocal(beta, beta))
                dve.wait_ge(sm_act, 2 * layer + 2)
                link(v.scalar_tensor_tensor(out=spl, in0=dec, scalar=0.0, in1=spl, op0=ALU.max, op1=ALU.add))
                v.scalar_tensor_tensor(out=dec, in0=spl, scalar=-1.0, in1=rowp[:, NDEC:].unsqueeze(1).to_broadcast([P, NT, NDEC]),
                                       op0=ALU.mult, op1=ALU.mult).then_inc(sm_dve, 1)
                blocks = na_blocks(layer)
                units = [(b, h) for b in range(len(blocks)) for h in range(4)]
                for gi in range(2):
                    G = 2 * layer + gi
                    for c in range(4):
                        dve.wait_ge(na_rs, 4 * G + c + 1)
                        gain = qg8[:, 0:1] if c < 2 else col(layer, "kg")
                        v.scalar_tensor_tensor(out=naq[:, c], in0=naq[:, c], scalar=gain, in1=nars[:, c % 2], op0=ALU.mult, op1=ALU.mult).then_inc(na_qk, 1)
                    u0 = na_u0(layer, gi)
                    b0 = u0 // 4
                    dve.wait_ge(na_bias, G + 1)

                    def outp(b):
                        dve.wait_ge(na_PV, u0 + 4 * b + 4)
                        hc = b % 2 * 4
                        link(v.reciprocal(nast[:, 2, 0:4], nast[:, 1, hc:hc + 4]))
                        v.tensor_tensor(naO[:, b % 2].rearrange("p (h x) -> p h x", h=4),
                                        na_obank[b % 2][:, 0:256].rearrange("p (h x) -> p h x", h=4),
                                        bcast(nast[:, 2, 0:4], 64), ALU.mult).then_inc(na_O, 1)

                    for u, (b, h) in enumerate(units):
                        lat, i = blocks[b]
                        dve.wait_ge(na_S, u0 + u + 1)
                        sp_ = ps[4 + u % 2]
                        lo = 256
                        if lat:
                            link(v.tensor_tensor(sp_[:, 0:256], sp_[:, 0:256], nab[:, h, VAR[i]], ALU.add))
                            lo = 0
                        link(v.reduce_max(nast[:, 0, 2 + u % 2:3 + u % 2], sp_[:, lo:512], AX.X))
                        if u >= 2:
                            dve.wait_ge(na_P, u0 + u - 1)
                        v.tensor_scalar(nast[:, 0, u % 2:u % 2 + 1], nast[:, 0, 2 + u % 2:3 + u % 2], -1.0, None, ALU.mult).then_inc(na_max, 1)
                        if h == 0 and b > 0:
                            outp(b - 1)
                    outp(len(blocks) - 1)
                for hg in range(2):
                    G = 2 * layer + hg
                    gq = 4 * layer + hg
                    if hg == 0:
                        dve.wait_ge(na_YA, (na_u0(layer, 1) + len(units)) // 4)
                    convs(layer, gq, rawp, cv, COL_AT["dncv"] + 30 * hg)
                    for c in range(4):
                        dve.wait_ge(dq_rs, 4 * G + c + 1)
                        q = QK[:, c]
                        v.tensor_tensor(q, q, rsb[:, c % 2], ALU.mult).then_inc(dq_n, 1)
                        dve.wait_ge(dq_n, 4 * G + c + 1)
                        dve.wait_ge(dq_rot, 4 * G + c + 1)
                        tmp = rsb[:, c % 2, 0:LAT]
                        link(v.tensor_tensor(tmp, ps[4 + 2 * (c % 2)], sin, ALU.mult))
                        link(v.tensor_tensor(q[:, CTX:], q[:, CTX:], cos, ALU.mult))
                        v.tensor_tensor(q[:, CTX:], q[:, CTX:], tmp, ALU.add).then_inc(dq_rope, 1)
                    dve.wait_ge(tr_copied, 6 * (gq + 1))
                    for d in range(2):
                        link(v.memset(dnS[:, d].rearrange("p g v -> p (g v)"), 0.0))
                    for n in range(6):
                        s = 6 * G + n
                        for d in range(2):
                            dve.wait_ge(dpe[d].sem, dpe[d].at(s, "GQ"))
                            dve.wait_ge(dpool[d].sem, dpool[d].at(s, "DM"))
                            for e in range(2):
                                ins = v.tensor_tensor(dMT[d][:, e::2], ps[4 * d + 1 + e][:, 0:256].rearrange("p (h x) -> p h x", h=2), dDM[d][:, e::2], ALU.mult)
                            ins.then_inc(ddve[d].sem, 1)
                            dve.wait_ge(dpe[d].sem, dpe[d].at(s, "GQ"))
                            dve.wait_ge(dpool[d].sem, dpool[d].at(s, "DA"))
                            for e in range(2):
                                ins = v.tensor_tensor(dAT[d][:, e::2], ps[4 * d + 1 + e][:, 256:512].rearrange("p (h x) -> p h x", h=2), dDA[d][:, e::2], ALU.mult)
                            ins.then_inc(ddve[d].sem, 1)
                        for d in range(2):
                            dve.wait_ge(ddve[d].sem, ddve[d].at(s, "MT"))
                            link(v.tensor_tensor(dXT[d], dMT[d], over(C[("um0", "lm0")[d]], 4), ALU.mult))
                            v.tensor_tensor(dXT[d], over(C["ident"], 4), dXT[d], ALU.subtract).then_inc(ddve[d].sem, 1)
                        for l in LV:
                            for d in range(2):
                                dve.wait_ge(dpe[d].sem, dpe[d].at(s, f"Y{l}"))
                                v.tensor_tensor(dY[d], ps[4 * d].rearrange("p (h x) -> p h x", h=4), over(C[f"{'lu'[d]}m{l}"], 4), ALU.mult).then_inc(ddve[d].sem, 1)
                            for d in range(2):
                                dve.wait_ge(dpe[d].sem, dpe[d].at(s, f"Z{l}"))
                                x = flat(dX[d] if l < 6 else dXT[d])
                                v.tensor_tensor(x, x, ps[4 * d + 1], ALU.subtract).then_inc(ddve[d].sem, 1)
                        for d in range(2):
                            t = TILES[d][n]
                            bc = 8 * d + 4 * hg
                            dve.wait_ge(dpe[d].sem, dpe[d].at(s, "V"))
                            v.tensor_tensor(dVN[d], ps[4 * d + 1][:, 0:256].rearrange("p (h x) -> p h x", h=4),
                                            bcast(beta[:, t, bc:bc + 4], 64), ALU.mult).then_inc(ddve[d].sem, 1)
                        for d in range(2):
                            t = TILES[d][n]
                            c0 = dec_col("dn", d, 4 * hg)
                            dve.wait_ge(dpe[d].sem, dpe[d].at(s, "ST"))
                            o = dno[:, t].rearrange("p (h x) -> p h x", h=4)
                            tmp = o if first_visit(n) else dTmp[d]
                            link(v.tensor_tensor(tmp, ps[4 * d + 2][:, 0:256].rearrange("p (h x) -> p h x", h=4),
                                                 bcast(EXX[:, t, 0, c0:c0 + 4], 64), ALU.mult))
                            if not first_visit(n):
                                link(v.tensor_tensor(o, o, tmp, ALU.add))
                            v.tensor_tensor(dno[:, t], dno[:, t], ps[4 * d + 3][:, 0:256], ALU.add).then_inc(ddve[d].sem, 1)
                            for h in range(4):
                                sl = slice(64 * (h % 2), 64 * (h % 2) + 64)
                                st = dnS[sl, d, h // 2, sl]
                                ins = v.scalar_tensor_tensor(out=st, in0=st, scalar=EXX[sl, t, 2, c0 + h:c0 + h + 1],
                                                             in1=ps[4 * d + 3][sl, 256 + h * 64:256 + h * 64 + 64], op0=ALU.mult, op1=ALU.add)
                            ins.then_inc(ddve[d].sem, 1)
                    dve.wait_ge(ddve[1].sem, ddve[1].at(6 * G + 5, "O"))
                    dve.wait_ge(ddve[0].sem, ddve[0].at(6 * G + 5, "O"))
                    of = dno.rearrange("p t c -> p (t c)")
                    link(v.tensor_tensor(dn_scr, of, of, ALU.mult))
                    v.reduce_sum(smt[:, 0:24], dn_scr.rearrange("p (g x) -> p g x", x=64), AX.X).then_inc(dn_ss, 1)
                    dve.wait_ge(dn_rs, G + 1)
                    v.tensor_tensor(of.rearrange("p (g x) -> p g x", x=64), of.rearrange("p (g x) -> p g x", x=64),
                                    bcast(smt[:, 0:24], 64), ALU.mult).then_inc(dn_on, 1)
                    dve.wait_ge(dn_ot, G + 1)
                    for c in range(2):
                        for i, (o, w) in enumerate(SEGS):
                            ins = v.scalar_tensor_tensor(out=YB[:, 2 * hg + c, o:o + w], in0=ps[4 + 2 * c + i][:, 0:w], scalar=col(layer, "dng"),
                                                         in1=zb[:, c, o:o + w], op0=ALU.mult, op1=ALU.mult)
                    ins.then_inc(dn_y, 1)
                for sg in range(2):
                    G = 2 * layer + sg
                    gq = 4 * layer + 2 + sg
                    convs(layer, gq, srawp, scvb, COL_AT["sscv"] + 30 * sg)
                    dve.wait_ge(tr_copied, 6 * (gq + 1))
                    link(v.memset(ssH.rearrange("p d x -> p (d x)"), 0.0))
                    for n in range(6):
                        s = 6 * G + n
                        for d in range(2):
                            t = TILES[d][n]
                            c0 = dec_col("ss", d, 8 * sg)
                            dve.wait_ge(spe[d].sem, spe[d].at(s, "CB"))
                            v.tensor_tensor(sCB[d], ps[4 * d + 2][:, 0:P], C[("le", "ge")[d]], ALU.mult).then_inc(sdve[d].sem, 1)
                            v.tensor_tensor(sXD[d].rearrange("p (h x) -> p h x", h=8), xt[:, t].rearrange("p (h x) -> p h x", h=8),
                                            bcast(spl[:, t, c0:c0 + 8], 64), ALU.mult).then_inc(sdve[d].sem, 1)
                        for half in range(2):
                            for d in range(2):
                                dve.wait_ge(sact[d].sem, sact[d].at(s, f"D{half}"))
                                dve.wait_ge(sdve[d].sem, sdve[d].at(s, "CBM"))
                                w = sW[d].rearrange("p (h x) -> p h x", h=4)
                                v.tensor_tensor(w, w, over(sCB[d], 4), ALU.mult).then_inc(sdve[d].sem, 1)
                        for d in range(2):
                            t = TILES[d][n]
                            c0 = dec_col("ss", d, 8 * sg)
                            dve.wait_ge(spe[d].sem, spe[d].at(s, "ST"))
                            tmp = yt[:, t] if first_visit(n) else sXD[d]
                            link(v.tensor_tensor(tmp.rearrange("p (h x) -> p h x", h=8), ps[4 * d].rearrange("p (h x) -> p h x", h=8),
                                                 bcast(EXX[:, t, 0, c0:c0 + 8], 64), ALU.mult))
                            if not first_visit(n):
                                link(v.tensor_tensor(yt[:, t], yt[:, t], tmp, ALU.add))
                            v.tensor_tensor(yt[:, t], yt[:, t], ps[4 * d + 3], ALU.add).then_inc(sdve[d].sem, 1)
                            hh = ssH[:, d].rearrange("p (h x) -> p h x", h=8)
                            link(v.tensor_tensor(hh, hh, bcast(EXX[:, t, 2, c0:c0 + 8], 64), ALU.mult))
                            v.tensor_tensor(ssH[:, d], ssH[:, d], ps[4 * d + 1], ALU.add).then_inc(sdve[d].sem, 1)
                    for c in range(4):
                        j = job(layer, f"ss{sg}", 6 + c)
                        dve.wait_ge(dense_free[j % 2], free_count(j))
                    for t in range(NT):
                        dve.wait_ge(ss_ot, NT * G + t + 1)
                        tk = slice(t * P, (t + 1) * P)
                        for c in range(4):
                            ins = v.scalar_tensor_tensor(out=YC[:, 4 * sg + c, tk], in0=YC[:, 4 * sg + c, tk], scalar=col(layer, "ssd", 4 * sg + c),
                                                         in1=ps[4 + t % 4][:, c * P:(c + 1) * P], op0=ALU.mult, op1=ALU.add)
                        link(ins)
                        v.tensor_tensor(YC[:, 4 * sg:4 * sg + 4, tk], YC[:, 4 * sg:4 * sg + 4, tk], szb[:, :, tk], ALU.mult).then_inc(ss_yz, 1)
                    dve.wait_ge(ss_rs, G + 1)
                    for c in range(4):
                        y = YC[:, 4 * sg + c]
                        ins = v.scalar_tensor_tensor(out=y, in0=y, scalar=col(layer, "ssg", 4 * sg + c), in1=srs, op0=ALU.mult, op1=ALU.mult)
                    ins.then_inc(ss_y, 1)
                lo, hi = (0, T) if len(segs) == 2 else (CTX, T)
                for m in range(4):
                    for br in range(3):
                        for c in range(2):
                            j = job(layer, "merge", 12 * m + 6 + 2 * br + c)
                            jg = job(layer, "merge", 12 * m + 2 * br + c)
                            dve.wait_ge(dense_free[jg % 2], free_count(jg))
                            dve.wait_ge(dense_done, j + 1)
                            dst = mt[:, 2 * m + c] if br == 0 else mtmp
                            for i, (o, w) in enumerate(segs):
                                ins = v.tensor_tensor(dst[:, o:o + w], ps[2 * (j % 2) + i][:, 0:w], gates[:, 2 * br + c, o:o + w], ALU.mult)
                            ins.then_inc(dense_free[j % 2], 1)
                            if br:
                                dve.wait_ge(dense_free[j % 2], free_count(j))
                                ins = v.tensor_tensor(mt[:, 2 * m + c, lo:hi], mt[:, 2 * m + c, lo:hi], mtmp[:, lo:hi], ALU.add)
                                if br == 2:
                                    ins.then_inc(m_ready, 1)
                                    dve.wait_ge(m_ready, KC * layer + 2 * m + c + 1)
                                else:
                                    link(ins)

                def residual(stage, part):
                    for c in range(KC):
                        j = job(layer, stage, c)
                        dve.wait_ge(dense_done, j + 1)
                        for i, (o, w) in enumerate(segs):
                            ins = v.scalar_tensor_tensor(out=X[:, c, o:o + w], in0=ps[2 * (j % 2) + i][:, 0:w], scalar=mod[:, part + c, i:i + 1],
                                                         in1=X[:, c, o:o + w], op0=ALU.mult, op1=ALU.add)
                        ins.then_inc(x_ready, 1)

                residual("out", 16)
                norm(2 * layer + 1, segs, 1)
                for c in range(FF // P):
                    j = job(layer, "ff1", c)
                    dve.wait_ge(dense_free[j % 2], free_count(j))
                    hc = hid[:, c, lo:hi]
                    v.tensor_tensor(hc, hc, hc, ALU.mult).then_inc(hid_ready, 1)
                residual("ff2", 40)

        @block.tensor
        def _(pe):
            mm, tr = nc.tensor.matmul, nc.tensor.transpose
            panel = [0]

            def slot():
                n = panel[0]
                panel[0] += 1
                pe.wait_ge(slot_full[n % RING], 16 * (n // RING + 1))
                return ring[:, n % RING * PANEL:(n % RING + 1) * PANEL]

            def dense(j, parts, segs, free=None):
                if free:
                    pe.wait_ge(*free)
                else:
                    pe.wait_ge(dense_free[j % 2], j // 2)
                for i, (o, w) in enumerate(segs):
                    for k, (wt, rows) in enumerate(parts):
                        ins = mm(ps[2 * (j % 2) + i][:, 0:w], wt, rows[:, o:o + w], start=(k == 0), stop=(k == len(parts) - 1))
                ins.then_inc(dense_done, 1)

            def from_h(j, p, c, segs):
                w = p.rearrange("p (k c) -> p k c", k=KC)
                dense(j, [(w[:, k, c * P:(c + 1) * P], H[:, k]) for k in range(KC)], segs, free_of(j))

            def free_of(j):
                r = j % NJOB
                layer = j // NJOB
                prev = j - 2
                if prev < 0:
                    return (h_ready, 1)
                rp = prev % NJOB
                lay = prev // NJOB
                if JOB_AT["out"] <= rp < JOB_AT["ff1"]:
                    return (x_ready, 2 * KC * lay + rp - JOB_AT["out"] + 1)
                if JOB_AT["ff2"] <= rp:
                    return (x_ready, 2 * KC * lay + KC + rp - JOB_AT["ff2"] + 1)
                return (dense_free[prev % 2], free_count(prev))

            def norm(q, segs):
                for k in range(KC):
                    pe.wait_ge(sq_ready, KC * q + k + 1)
                    for i, (o, w) in enumerate(segs):
                        ins = mm(ps[i][:, 0:w], C["ones"], nsq[:, k % 2, o:o + w], start=(k == 0), stop=(k == KC - 1))
                    ins.then_inc(nsum_ready, 1)
                pe.wait_ge(h_ready, q + 1)

            pe.wait_ge(cst_in, 16)
            pe.wait_ge(scv_ready, 1)
            for layer in range(DEPTH):
                segs = segs_of(layer)
                for i in range(ADA_P):
                    w = slot().rearrange("p (k c) -> p k c", k=KC)
                    for c in range(2):
                        f = 2 * i + c
                        for k in range(KC):
                            ins = mm(ps[7][:, 2 * f:2 * f + 2], w[:, k, c * P:(c + 1) * P], scv[:, k], start=(k == 0), stop=(k == KC - 1))
                    ins.then_inc(ada_done, 1)
                norm(2 * layer, SEGS)
                pe.wait_ge(wsm_in, 16 * (layer + 1))
                for t in range(NT):
                    for k in range(KC):
                        ins = mm(ps[6][:, t * NSM:(t + 1) * NSM], H[:, k, t * P:(t + 1) * P], wsm[:, k], start=(k == 0), stop=(k == KC - 1))
                ins.then_inc(sm_done, 1)
                pe.wait_ge(sm_dve, 2 * layer + 2)
                for t in range(NT):
                    bank, at = ps[4 + t // 3], t % 3 * 3 * NDEC
                    for e, (f, b) in enumerate((("le", "ge"), ("gt", "lt"))):
                        mm(bank[:, at + e * NDEC:at + e * NDEC + 24], C[f], dec[:, t, 0:24], start=True, stop=True)
                        mm(bank[:, at + e * NDEC + 24:at + (e + 1) * NDEC], C[b], dec[:, t, 24:48], start=True, stop=True)
                    ins = mm(bank[:, at + 2 * NDEC:at + 3 * NDEC], C["ones"], dec[:, t], start=True, stop=True)
                ins.then_inc(cum_done, 1)
                pe.wait_ge(exx_ready, layer + 1)
                blocks = na_blocks(layer)
                units = [(b, h) for b in range(len(blocks)) for h in range(4)]
                for gi in range(2):
                    G = 2 * layer + gi

                    def headsum(c):
                        pe.wait_ge(na_sq, 4 * G + c + 1)
                        if c >= 2:
                            pe.wait_ge(na_rs, 4 * G + c - 1)
                        for i, (o, w) in enumerate(SEGS):
                            ins = mm(ps[4 + 2 * (c % 2) + i][:, 0:w], C["bones"], nasq[:, c % 2, o:o + w], start=True, stop=True)
                        ins.then_inc(na_ss, 1)

                    for i in range(3):
                        p = slot()
                        for c in range(2):
                            ch = 2 * i + c
                            from_h(job(layer, f"na{gi}", ch), p, c, SEGS)
                            if 1 <= ch <= 4:
                                headsum(ch - 1)
                    pe.wait_ge(na_rs, 4 * G + 4)
                    jv = job(layer, f"na{gi}", 5)
                    pe.wait_ge(dense_free[jv % 2], free_count(jv))
                    pe.wait_ge(dense_free[(jv - 1) % 2], free_count(jv - 1))
                    for i in range(5):
                        if i == 4:
                            pe.wait_ge(na_vc, 5 * G + 1)
                        for half in range(2):
                            for c in range(2):
                                if i == 0:
                                    src = nav[:, c, half * P:(half + 1) * P]
                                else:
                                    at = CTX + window(i - 1) * GR + half * P
                                    src = nav[:, c, at:at + P]
                                ins = tr(ps[4 + i % 4][:, half * 256 + c * P:half * 256 + (c + 1) * P], src, C["ident"])
                        ins.then_inc(na_vt, 1)
                    pe.wait_ge(na_vc, 5 * G + 5)
                    pe.wait_ge(na_qk, 4 * G + 4)
                    u0 = na_u0(layer, gi)
                    b0 = u0 // 4

                    def scores(u):
                        b, h = units[u]
                        lat, i = blocks[b]
                        if u >= 2:
                            pe.wait_ge(na_P, u0 + u - 1)
                        hs = slice(64 * (h % 2), 64 * (h % 2) + 64)
                        q, k = naq[hs, h // 2], naq[hs, 2 + h // 2]
                        at = (CTX if lat else 0) + i * P
                        qs = q[:, at:at + P]
                        ins = mm(ps[4 + u % 2][:, 256:512], qs, k[:, 0:CTX], start=True, stop=True)
                        if lat:
                            ins = mm(ps[4 + u % 2][:, 0:256], qs, nak(k[:, CTX:], i), start=True, stop=True)
                        ins.then_inc(na_S, 1)

                    def back(b):
                        pe.wait_ge(na_O, b0 + b + 1)
                        if b >= 2:
                            pe.wait_ge(na_YA, b0 + b - 1)
                        for c in range(2):
                            ins = tr(na_tbank[b % 2][:, c * P:(c + 1) * P], naO[:, b % 2, c * P:(c + 1) * P], C["ident"])
                        ins.then_inc(na_OT, 1)

                    scores(0)
                    for u, (b, h) in enumerate(units):
                        if u + 1 < len(units):
                            scores(u + 1)
                        lat, i = blocks[b]
                        pe.wait_ge(na_P, u0 + u + 1)
                        if u:
                            pe.wait_ge(na_PT, u0 + u)
                        chunks = range(4) if lat else range(2, 4)
                        for c in chunks:
                            ins = tr(ps[6][:, c * P:(c + 1) * P], naP[:, u % 2, c * P:(c + 1) * P], C["ident"])
                        ins.then_inc(na_T, 1)
                        pe.wait_ge(na_PT, u0 + u + 1)
                        if h == 0 and b >= 2:
                            pe.wait_ge(na_O, b0 + b - 1)
                        for n, c in enumerate(chunks):
                            tile = c - 2 if c >= 2 else 2 + 2 * i + c
                            ins = mm(na_obank[b % 2][:, h * 64:(h + 1) * 64], naPT[:, u % 2, c * P:(c + 1) * P], navt[:, tile, h * 64:(h + 1) * 64],
                                     start=(n == 0), stop=(n == len(chunks) - 1))
                        ins.then_inc(na_PV, 1)
                        if h == 0 and b > 0:
                            back(b - 1)
                    back(len(blocks) - 1)
                    pe.wait_ge(na_YA, b0 + len(blocks))
                for hg in range(2):
                    G = 2 * layer + hg
                    gq = 4 * layer + hg
                    for i in range(4):
                        p = slot()
                        for c in range(2):
                            from_h(job(layer, f"dn{hg}", 2 * i + c), p, c, SEGS)
                    for c in range(5):
                        if c < 4:
                            pe.wait_ge(dq_sq, 4 * G + c + 1)
                            if c >= 2:
                                pe.wait_ge(dq_rope, 4 * G + c - 1)
                            for i, (o, w) in enumerate(SEGS):
                                ins = mm(ps[4 + 2 * (c % 2) + i][:, 0:w], C["bones"], sqb[:, c % 2, o:o + w], start=True, stop=True)
                            ins.then_inc(dq_ss, 1)
                            pe.wait_ge(dq_n, 4 * G + c + 1)
                            mm(ps[4 + 2 * (c % 2)][:, :], C["rot"], QK[:, c, CTX:], start=True, stop=True).then_inc(dq_rot, 1)
                    pe.wait_ge(dq_rope, 4 * G + 4)
                    pe.wait_ge(silu_done, 6 * gq + 6)
                    for t in range(NT):
                        if t >= 4:
                            pe.wait_ge(tr_copied, 6 * gq + t - 3)
                        tk = slice(t * P, (t + 1) * P)
                        for c, src in enumerate((QK[:, 2], QK[:, 3], dnV[:, 0], dnV[:, 1])):
                            ins = tr(ps[4 + t % 4][:, c * P:(c + 1) * P], src[:, tk], C["ident"])
                        ins.then_inc(tr_done, 1)
                    pe.wait_ge(tr_copied, 6 * gq + 6)
                    for z in (7, 6):
                        j = job(layer, f"dn{hg}", z)
                        pe.wait_ge(dense_free[j % 2], free_count(j))
                    hs = [slice(64 * (h % 2), 64 * (h % 2) + 64) for h in range(4)]

                    def each(bank, lhs, rhs):
                        for h in range(4):
                            ins = mm(bank[:, h * P:(h + 1) * P], lhs(h), rhs(h), start=True, stop=True)
                        return ins

                    for n in range(6):
                        s = 6 * G + n
                        for d in range(2):
                            B = ps[4 * d:4 * d + 4]
                            pe.wait_ge(dpool[d].sem, dpool[d].at(s, "R"))
                            if n:
                                pe.wait_ge(ddve[d].sem, ddve[d].at(s - 1, "S"))
                            mm(B[0], C[("gt", "lt")[d]], flat(dR[d]), start=True, stop=True).then_inc(dpe[d].sem, 1)
                            t = TILES[d][n]
                            tk = slice(t * P, (t + 1) * P)
                            for qk, at in ((2, 0), (0, 256)):
                                for h in range(4):
                                    o = at + h // 2 * P
                                    ins = mm(B[1 + h % 2][:, o:o + P], QK[hs[h], 2 + h // 2, tk], QK[hs[h], qk + h // 2, tk], start=True, stop=True)
                                ins.then_inc(dpe[d].sem, 1)
                        for d in range(2):
                            B = ps[4 * d:4 * d + 4]
                            pe.wait_ge(ddve[d].sem, ddve[d].at(s, "XT1"))
                            for h in range(4):
                                ins = tr(B[2][:, h * P:(h + 1) * P], dXT[d][:, h], C["ident"])
                            ins.then_inc(dpe[d].sem, 1)
                        for l in LV:
                            for d in range(2):
                                B = ps[4 * d:4 * d + 4]
                                if l == 1:
                                    pe.wait_ge(dact[d].sem, dact[d].at(s, "X1"))
                                else:
                                    pe.wait_ge(ddve[d].sem, ddve[d].at(s, f"X{l - 1}"))
                                each(B[0], lambda h: dMT[d][:, h], lambda h: dX[d][:, h]).then_inc(dpe[d].sem, 1)
                            for d in range(2):
                                B = ps[4 * d:4 * d + 4]
                                pe.wait_ge(ddve[d].sem, ddve[d].at(s, f"Y{l}"))
                                if l > 1:
                                    pe.wait_ge(dact[d].sem, dact[d].at(s, f"XT{l - 1}"))
                                if l < 6:
                                    each(B[1], lambda h: dXT[d][:, h], lambda h: dY[d][:, h]).then_inc(dpe[d].sem, 1)
                                else:
                                    each(B[1], lambda h: dY[d][:, h], lambda h: dXT[d][:, h]).then_inc(dpe[d].sem, 1)
                            if l < 6:
                                for d in range(2):
                                    B = ps[4 * d:4 * d + 4]
                                    pe.wait_ge(ddve[d].sem, ddve[d].at(s, f"X{l}"))
                                    for h in range(4):
                                        ins = tr(B[2][:, h * P:(h + 1) * P], dX[d][:, h], C["ident"])
                                    ins.then_inc(dpe[d].sem, 1)
                        for d in range(2):
                            B = ps[4 * d:4 * d + 4]
                            pe.wait_ge(ddve[d].sem, ddve[d].at(s, "X6"))
                            pe.wait_ge(dpool[d].sem, dpool[d].at(s, "KE"))
                            for h in range(4):
                                ins = mm(B[0][hs[h], h // 2 * P:(h // 2 + 1) * P], dKE[d][:, h], dXT[d][:, h], start=True, stop=True)
                            ins.then_inc(dpe[d].sem, 1)
                        for d in range(2):
                            B = ps[4 * d:4 * d + 4]
                            t = TILES[d][n]
                            tk = slice(t * P, (t + 1) * P)
                            pe.wait_ge(dact[d].sem, dact[d].at(s, "WT"))
                            for g in range(2):
                                mm(B[1][:, g * P:(g + 1) * P], dWT[d][:, g], dnS[:, d, g], start=True, stop=False)
                                for h in (2 * g, 2 * g + 1):
                                    ins = mm(B[1][:, h * 64:h * 64 + 64], dXT[d][:, h], kvt[:, t, 256 + h * 64:256 + (h + 1) * 64],
                                             start=False, stop=h % 2 == 1)
                            ins.then_inc(dpe[d].sem, 1)
                            for g in range(2):
                                ins = mm(B[2][:, g * P:(g + 1) * P], QK[:, g, tk], dnS[:, d, g], start=True, stop=True)
                            ins.then_inc(dpe[d].sem, 1)
                        for d in range(2):
                            B = ps[4 * d:4 * d + 4]
                            pe.wait_ge(ddve[d].sem, ddve[d].at(s, "VN"))
                            for h in range(4):
                                ins = mm(B[3][:, h * 64:(h + 1) * 64], dAT[d][:, h], dVN[d][:, h], start=True, stop=True)
                            ins.then_inc(dpe[d].sem, 1)
                            pe.wait_ge(dpool[d].sem, dpool[d].at(s, "KD"))
                            for g in range(2):
                                ins = mm(B[3][:, 256 + g * P:256 + (g + 1) * P], flat(dKD[d])[:, g * P:(g + 1) * P], flat(dVN[d])[:, g * P:(g + 1) * P],
                                         start=True, stop=True)
                            ins.then_inc(dpe[d].sem, 1)
                    pe.wait_ge(dn_on, G + 1)
                    for c in range(2):
                        for t in range(NT):
                            bank, at = (ps[4 + 2 * c], (t - 2) * P) if t >= 2 else (ps[5 + 2 * c], t * P)
                            ins = tr(bank[:, at:at + P], dno[:, t, c * P:(c + 1) * P], C["ident"])
                    ins.then_inc(dn_ot, 1)
                    pe.wait_ge(dn_y, G + 1)
                for sg in range(2):
                    G = 2 * layer + sg
                    gq = 4 * layer + 2 + sg
                    for i in range(3):
                        p = slot()
                        for c in range(2):
                            from_h(job(layer, f"ss{sg}", 2 * i + c), p, c, SEGS)
                    pe.wait_ge(silu_done, 6 * gq + 6)
                    for t in range(NT):
                        if t >= 2:
                            pe.wait_ge(tr_copied, 6 * gq + t - 1)
                        tk = slice(t * P, (t + 1) * P)
                        for c in range(4):
                            tr(ps[4 + t % 2][:, c * P:(c + 1) * P], YC[:, 4 * sg + c, tk], C["ident"])
                        tr(ps[6 + t % 2][:, 0:P], BC[:, 0, tk], C["ident"]).then_inc(tr_done, 1)
                    pe.wait_ge(tr_copied, 6 * gq + 6)
                    for n in range(6):
                        s = 6 * G + n
                        for d in range(2):
                            B = ps[4 * d:4 * d + 4]
                            t = TILES[d][n]
                            tk = slice(t * P, (t + 1) * P)
                            pe.wait_ge(spool[d].sem, spool[d].at(s, "R0"))
                            if n:
                                pe.wait_ge(sdve[d].sem, sdve[d].at(s - 1, "H"))
                            mm(B[0], C[("gt", "lt")[d]], sR[d], start=True, stop=True).then_inc(spe[d].sem, 1)
                            mm(B[2][:, 0:P], BC[:, 0, tk], BC[:, 1, tk], start=True, stop=True).then_inc(spe[d].sem, 1)
                            pe.wait_ge(spool[d].sem, spool[d].at(s, "R1"))
                            mm(B[1], C[("gt", "lt")[d]], sR[d], start=True, stop=True).then_inc(spe[d].sem, 1)
                        for half in range(2):
                            for d in range(2):
                                B = ps[4 * d:4 * d + 4]
                                pe.wait_ge(sdve[d].sem, sdve[d].at(s, f"W{half}"))
                                for h in range(4):
                                    at = (4 * half + h) * 64
                                    ins = mm(B[3][:, at:at + 64], sW[d][:, h * P:(h + 1) * P], sXD[d][:, at:at + 64], start=True, stop=True)
                                ins.then_inc(spe[d].sem, 1)
                        for d in range(2):
                            B = ps[4 * d:4 * d + 4]
                            t = TILES[d][n]
                            tk = slice(t * P, (t + 1) * P)
                            mm(B[0], BC[:, 1, tk], ssH[:, d], start=True, stop=True).then_inc(spe[d].sem, 1)
                            pe.wait_ge(spool[d].sem, spool[d].at(s, "XW"))
                            mm(B[1], bt[:, t], sR[d], start=True, stop=True).then_inc(spe[d].sem, 1)
                    for d in range(2):
                        pe.wait_ge(sdve[d].sem, sdve[d].at(6 * G + 5, "H"))
                    for t in range(NT):
                        if t >= 4:
                            pe.wait_ge(ss_yz, NT * G + t - 3)
                        for c in range(4):
                            ins = tr(ps[4 + t % 4][:, c * P:(c + 1) * P], yt[:, t, c * P:(c + 1) * P], C["ident"])
                        ins.then_inc(ss_ot, 1)
                        if t == 3:
                            for i in range(2):
                                p = slot()
                                for c in range(2):
                                    from_h(job(layer, f"ss{sg}", 6 + 2 * i + c), p, c, SEGS)
                    for c in range(4):
                        pe.wait_ge(ss_sq, 4 * G + c + 1)
                        for i, (o, w) in enumerate(SEGS):
                            ins = mm(ps[4 + i][:, 0:w], C["ones"], ssq[:, c, o:o + w], start=(c == 0), stop=(c == 3))
                    ins.then_inc(ss_sum, 1)
                    pe.wait_ge(ss_rs, G + 1)
                for m in range(4):
                    for br in range(3):
                        p = slot()
                        for c in range(2):
                            from_h(job(layer, "merge", 12 * m + 2 * br + c), p, c, segs)
                    pe.wait_ge(ss_y, 2 * (layer + 1))
                    w = slot().rearrange("p (k c) -> p k c", k=KC)
                    for br, Y in ((0, YA), (1, YB), (2, YC)):
                        if br == 2:
                            w = slot().rearrange("p (k c) -> p k c", k=KC)
                        for c in range(2):
                            j = job(layer, "merge", 12 * m + 6 + 2 * br + c)
                            k0, nk = (0, 4, 0)[br], (4, 4, 8)[br]
                            dense(j, [(w[:, k0 + k, c * P:(c + 1) * P], Y[:, k]) for k in range(nk)], segs, free_of(j))
                pe.wait_ge(m_ready, KC * (layer + 1))
                for i in range(4):
                    w = slot().rearrange("p (k c) -> p k c", k=KC)
                    for c in range(2):
                        j = job(layer, "out", 2 * i + c)
                        dense(j, [(w[:, k, c * P:(c + 1) * P], mt[:, k]) for k in range(KC)], segs, free_of(j))
                norm(2 * layer + 1, segs)
                for i in range(FF // 256):
                    p = slot()
                    for c in range(2):
                        from_h(job(layer, "ff1", 2 * i + c), p, c, segs)
                pe.wait_ge(hid_ready, FF // P * (layer + 1))
                for c in range(KC):
                    parts = []
                    for half in range(2):
                        w = slot().rearrange("p (k c) -> p k c", k=16)
                        parts += [(w[:, k], hid[:, 16 * half + k]) for k in range(16)]
                    j = job(layer, "ff2", c)
                    dense(j, parts, segs, free_of(j))


def _panels(w, cols=None, kc=KC, width=256):
    w = w if cols is None else w[:, cols]
    n = w.shape[1] // width
    a = w.reshape(-1, kc, P, n, width)
    return a.transpose(3, 0, 2, 1, 4).reshape(-1, P, PANEL)


def _cols(v):
    return np.asarray(v).reshape(-1, P).T


def kernel(**inputs):
    import concourse.bacc as _bacc
    from concourse.bass_utils import run_bass_kernel_spmd as _run

    a = {k: np.asarray(v) for k, v in inputs.items()}
    r = np.arange
    streams, cols, rows, small = [], [], [], []
    for l in range(DEPTH):
        w = a["w_in"][l]
        parts = [_panels(a["w_ada"][l])]
        for g in range(2):
            parts.append(_panels(w, np.concatenate([512 * i + 256 * g + r(256) for i in range(3)])))
        for g in range(2):
            parts.append(_panels(w, np.concatenate([1536 + 512 * i + 256 * g + r(256) for i in range(4)])))
        for g in range(2):
            xbc = 4640
            parts.append(_panels(w, np.concatenate([xbc + 512 * g + r(512), xbc + 1024 + 128 * g + r(128),
                                                    xbc + 1280 + 128 * g + r(128), 3616 + 512 * g + r(512)])))
        pab = np.concatenate([a["w_pa"][l], a["w_pb"][l]], axis=0)
        for m in range(4):
            c = 256 * m + r(256)
            parts.append(_panels(w, np.concatenate([6208 + D * i + c for i in range(3)])))
            parts += [_panels(pab, c), _panels(a["w_pc"][l], c)]
        parts += [_panels(a["w_out"][l]), _panels(a["w_ff1"][l]), _panels(a["w_ff2"][l], kc=16, width=P)]
        streams += parts
        order = np.concatenate([3584 + r(16), 3600 + r(8), 6176 + r(16), 3608 + r(8), 6192 + r(16)])
        small.append(w[:, order].reshape(KC, P, NSM).transpose(1, 0, 2))
        both = [np.concatenate([a[f"dn_{n}"][l][0], a[f"ssd_{n}"][l][0], a[f"dn_{n}"][l][1], a[f"ssd_{n}"][l][1]]) for n in ("dt_bias", "a_log")]
        rows.append(np.concatenate(both))
        cv = []
        for name, groups in (("dn_conv_w", [[2 * g, 2 * g + 1, 4 + 2 * g, 5 + 2 * g, 8 + 2 * g, 9 + 2 * g] for g in range(2)]),
                             ("ssd_conv_w", [[4 * g, 4 * g + 1, 4 * g + 2, 4 * g + 3, 8 + g, 10 + g] for g in range(2)])):
            t = a[name][l]
            for g in groups:
                for c in g:
                    cv.append(t[:, c * P:(c + 1) * P].T)
        sb_ = _cols(a["ssd_conv_b"][l])
        sscb = [sb_[:, [4 * g, 4 * g + 1, 4 * g + 2, 4 * g + 3, 8 + g, 10 + g]] for g in range(2)]
        cols.append(np.concatenate([
            _cols(a["b_ada"][l]), _cols(a["norm1_g"][l]), _cols(a["norm2_g"][l]), *cv, *sscb,
            _cols(np.tile(a["na_q_gain"][l], 2)), _cols(np.tile(a["na_k_gain"][l], 2)), _cols(np.tile(a["dn_o_gain"][l], 2)),
            _cols(np.repeat(a["ssd_d"][l], 64)), _cols(a["ssd_o_gain"][l])], axis=1))
    rpb = np.pad(a["na_rpb"], ((0, 0), (0, 0), (0, 0), (16, 17)))
    rpb = np.stack([rpb[..., 15 - i:15 - i + BIAS_W] for i in range(BLK_C)], axis=2)
    xs = np.concatenate([a["ctx"][0], a["x"][0]], axis=0).T.reshape(KC, P, T).transpose(1, 0, 2)
    cs = np.stack([_cols(a["c"][0]), _cols(a["c_ctx"])], axis=2)
    arrays = {"x_in": xs, "c_in": cs, "stream": np.concatenate(streams), "wsmall": np.stack(small), "cols": np.stack(cols),
              "rows": np.stack(rows), "rpb": rpb, "consts": constants()}
    arrays = {k: np.ascontiguousarray(v) for k, v in arrays.items()}
    nc = _bacc.Bacc("TRN2", target_bir_lowering=False, num_devices=1)
    args = [nc.dram_tensor(n, v.shape, F32, kind="ExternalInput").ap() for n, v in arrays.items()]
    out = nc.dram_tensor("out", (P, KC, LAT), F32, kind="ExternalOutput").ap()
    build(nc, *args, out)
    got = _run(nc, [arrays], core_ids=[0]).results[0]["out"]
    return np.ascontiguousarray(got.transpose(1, 0, 2).reshape(D, LAT).T)[None]
```

```python
import math

import numpy as np
import concourse.bass as bass
from concourse import mybir

F32 = mybir.dt.float32
ACT = mybir.ActivationFunctionType
ALU = mybir.AluOpType
AX = mybir.AxisListType

P = 128
D = 1024
KC = D // P
CTX, LAT = 256, 512
T = CTX + LAT
NT = T // P
DEPTH = 2
GW = 64
GR = LAT // GW
HD = 64
NAH, DNH, SSH = 8, 8, 16
WIN_C = 16
BLK_C = 16
BIAS_W = 48
FF = 4 * D
EPS = 1e-6
NEG = -1.0e30
SEGS = ((CTX, LAT), (0, CTX))
RAWW = T + 6
RAW0 = (2, CTX + 4)

RING = 4
PANEL = 2048

ADA_P = 6 * D // 256
ADA0 = 2 * D // 256
ADA_OUT = ADA0 + 12
PANELS = dict(ada=ADA_P, na0=3, na1=3, dn0=4, dn1=4, ss0=5, ss1=5, merge=20, out=4, ff1=FF // 256, ff2=2 * KC)
JOBS = dict(na0=6, na1=6, dn0=8, dn1=8, ss0=10, ss1=10, merge=48, out=KC, ff1=FF // P, ff2=KC)


def offsets(counts):
    at, out = 0, {}
    for name, n in counts.items():
        out[name] = at
        at += n
    return out, at


PANEL_AT, NPANEL = offsets(PANELS)
JOB_AT, NJOB = offsets(JOBS)

COLS = dict(n1=8, n2=8, dncv=60, sscv=60, sscb=12, qg=1, kg=1, dng=1, ssd=8, ssg=8)
COL_AT, NCOL = offsets(COLS)
NSM = 64
NDEC = 48


def dec_col(kind, d, h):
    return 24 * d + (h if kind == "dn" else 8 + h)


def level_masks():
    p = np.arange(P)[:, None]
    f = np.arange(P)[None, :]
    out = []
    for l in range(7):
        s = 1 << l
        out.append(((p // (2 * s) == f // (2 * s)) & (p // s % 2 == 1) & (f // s % 2 == 0)).astype(np.float32))
    return out


def constants():
    p = np.arange(P)[:, None]
    f = np.arange(P)[None, :]
    sq = [p == f, np.ones((P, P), bool), p // 64 == f // 64, p <= f, p >= f, p < f, p > f]
    sq = [a.astype(np.float32) for a in sq]
    rot = np.zeros((P, P), np.float32)
    for o in range(P):
        if o % 32 < 16:
            rot[o + 16, o] = -1.0
        else:
            rot[o - 16, o] = 1.0
    lm = level_masks()
    sq += [rot] + lm + [a.T for a in lm]
    square = np.concatenate(sq, axis=1)
    tok = np.arange(LAT)
    quarter = 16
    inv = (10000.0 ** (-np.arange(quarter, dtype=np.float32) / np.float32(quarter))).astype(np.float32)
    d = np.arange(P) % 64
    pos = np.where(d[:, None] < 32, tok[None, :] // GW, tok[None, :] % GW).astype(np.float32)
    ang = (pos * inv[d % 16][:, None]).astype(np.float32)
    trig = np.concatenate([np.cos(ang), np.sin(ang)], axis=1).astype(np.float32)
    nam = np.zeros((GR, BLK_C, 3, GR, 32), np.float32)
    for v, b in enumerate((0, 1, 3)):
        start = min(max(b * BLK_C - 8, 0), GW - 32)
        for i in range(BLK_C):
            w = min(max(b * BLK_C + i - WIN_C // 2, 0), GW - WIN_C) - start
            ok = np.zeros(32, bool)
            ok[w:w + WIN_C] = True
            nam[:, i, v] = np.where(ok, 0.0, NEG)
    return np.ascontiguousarray(np.concatenate([square, trig, nam.reshape(P, -1)], axis=1), dtype=np.float32)


SQ = ["ident", "ones", "bones", "le", "ge", "lt", "gt", "rot"] + [f"lm{i}" for i in range(7)] + [f"um{i}" for i in range(7)]
NCONST = len(SQ) * P + 2 * LAT + 3 * 256


class Steps:

    def __init__(self, sem, names):
        self.sem, self.names = sem, list(names)

    def at(self, step, name):
        return step * len(self.names) + self.names.index(name) + 1


def build(nc, x_in, c_in, stream, wsmall_in, cols_in, rows_in, rpb_in, const_in, bada_in_, out):
    def sb(name, n):
        return nc.alloc_sbuf_tensor(name, [P, n], F32)

    X = sb("X", KC * T)[:, :].rearrange("p (k t) -> p k t", k=KC)
    H = sb("H", KC * T)[:, :].rearrange("p (k t) -> p k t", k=KC)
    ring = sb("ring", RING * PANEL)
    cst = sb("cst", NCONST)
    C = {n: cst[:, i * P:(i + 1) * P] for i, n in enumerate(SQ)}
    cos = cst[:, len(SQ) * P:len(SQ) * P + LAT]
    sin = cst[:, len(SQ) * P + LAT:len(SQ) * P + 2 * LAT]
    nam = cst[:, len(SQ) * P + 2 * LAT:].rearrange("p (v x) -> p v x", v=3)
    prm = sb("prm", NCOL)
    rowp = sb("rowp", 2 * NDEC)
    cvec = sb("cvec", 2 * KC)[:, :].rearrange("p (k s) -> p k s", s=2)
    scv = sb("scv", 2 * KC)[:, :].rearrange("p (k s) -> p k s", s=2)
    mods = [sb(f"mod{l}", 96)[:, :].rearrange("p (f s) -> p f s", s=2) for l in range(DEPTH)]
    bada = sb("b_ada", 48 * DEPTH)
    am = sb("am", 16)[:, :].rearrange("p (f s) -> p f s", s=2)
    qg8 = sb("qg8", 1)
    wsm = sb("wsm", KC * NSM)[:, :].rearrange("p (k c) -> p k c", k=KC)
    beta = sb("beta", NT * 16)[:, :].rearrange("p (t c) -> p t c", t=NT)
    spl = sb("spl", NT * NDEC)[:, :].rearrange("p (t c) -> p t c", t=NT)
    dec = sb("dec", NT * NDEC)[:, :].rearrange("p (t c) -> p t c", t=NT)
    EXX = sb("EXX", 3 * NT * NDEC)[:, :].rearrange("p (t e c) -> p t e c", t=NT, e=3)
    smt = sb("smt", 24)
    eps_t, extra_t = sb("eps_t", 1), sb("extra_t", 1)
    arena_n = 25344
    ar = sb("arena", arena_n)
    top = [0]

    def take(n):
        a = ar[:, top[0]:top[0] + n]
        top[0] += n
        assert top[0] <= arena_n, top[0]
        return a

    YA = take(4 * T).rearrange("p (k t) -> p k t", k=4)
    YB = take(4 * T).rearrange("p (k t) -> p k t", k=4)
    mixer0 = top[0]

    naq = take(4 * T).rearrange("p (k t) -> p k t", k=4)
    nav = take(2 * T).rearrange("p (k t) -> p k t", k=2)
    nasq = take(2 * T).rearrange("p (k t) -> p k t", k=2)
    nars = take(2 * T).rearrange("p (k t) -> p k t", k=2)
    navt = take(10 * 256).rearrange("p (t c) -> p t c", t=10)
    nag = take(4 * GR * BIAS_W).rearrange("p (h r m) -> p h r m", h=4, r=GR)
    nab = take(4 * 3 * 256).rearrange("p (h v x) -> p h v x", h=4, v=3)
    naP = take(2 * 512).rearrange("p (b x) -> p b x", b=2)
    naPT = take(2 * 512).rearrange("p (b x) -> p b x", b=2)
    naO = take(2 * 256).rearrange("p (b x) -> p b x", b=2)
    nast = take(3 * 64).rearrange("p (s x) -> p s x", s=3)
    rpbp = take(64)

    top[0] = mixer0
    QK = take(4 * T).rearrange("p (k t) -> p k t", k=4)
    kvt = take(NT * 512).rearrange("p (t c) -> p t c", t=NT)
    zb = take(2 * T).rearrange("p (k t) -> p k t", k=2)
    dno = take(NT * 256).rearrange("p (t c) -> p t c", t=NT)
    dnS = take(2 * 256).rearrange("p (d g v) -> p d g v", d=2, g=2)
    after_o = top[0]
    dnV = take(2 * T).rearrange("p (k t) -> p k t", k=2)
    rawp = take(2 * RAWW).rearrange("p (b t) -> p b t", b=2)
    cv = take(2 * RAWW).rearrange("p (b t) -> p b t", b=2)
    sqb = take(2 * T).rearrange("p (b t) -> p b t", b=2)
    rsb = take(3 * T).rearrange("p (b t) -> p b t", b=3)
    top[0] = after_o

    def per_dir(n, h=4):
        return [take(n).rearrange("p (h x) -> p h x", h=h) for _ in range(2)]

    dR, dD = per_dir(512), per_dir(512)
    dDM, dMT, dX, dXT = per_dir(512), per_dir(512), per_dir(512), per_dir(512)
    dAT = per_dir(512)
    dY = per_dir(256)
    dKE, dKD = per_dir(256), per_dir(256)
    dVN = [x[:, 0:2].rearrange("p a (b x) -> p (a b) x", b=2) for x in dR]
    dTmp = [x[:, 0:2].rearrange("p a (b x) -> p (a b) x", b=2) for x in dX]
    dWT = per_dir(256, 2)
    dDA = dD

    top[0] = mixer0
    YC = take(8 * T).rearrange("p (k t) -> p k t", k=8)
    BC = take(2 * T).rearrange("p (k t) -> p k t", k=2)
    xt = take(NT * 512).rearrange("p (t c) -> p t c", t=NT)
    bt = take(NT * P).rearrange("p (t c) -> p t c", t=NT)
    yt = take(NT * 512).rearrange("p (t c) -> p t c", t=NT)
    ssH = take(2 * 512).rearrange("p (d x) -> p d x", d=2)
    after_h = top[0]
    srawp = take(2 * RAWW).rearrange("p (b t) -> p b t", b=2)
    scvb = take(2 * RAWW).rearrange("p (b t) -> p b t", b=2)
    top[0] = after_h
    sR = [take(512) for _ in range(2)]
    sCB = [take(128) for _ in range(2)]
    sXD = [take(512) for _ in range(2)]
    sW = [take(512) for _ in range(2)]
    szb = xt.rearrange("p t c -> p (t c)").rearrange("p (k t) -> p k t", k=4)
    ssq = yt.rearrange("p t c -> p (t c)").rearrange("p (k t) -> p k t", k=4)
    srs = bt.rearrange("p t c -> p (t c)")
    top[0] = mixer0 + 8 * T
    gates = take(6 * T).rearrange("p (k t) -> p k t", k=6)
    mt = take(8 * T).rearrange("p (k t) -> p k t", k=8)
    mtmp = take(T)
    top[0] = 0
    nsq = take(2 * T).rearrange("p (b t) -> p b t", b=2)
    nrs = take(T)
    top[0] = 0
    hid = take(FF // P * T).rearrange("p (k t) -> p k t", k=FF // P)

    ps = [nc.alloc_psum_tensor(f"ps{i}", [P, 512], F32)[:, :] for i in range(8)]

    na_sbank, na_obank, na_tbank, ada_bank = (ps[4], ps[5], ps[1]), (ps[7], ps[3]), ps[2], ps[0]

    dn_scr = ar[:, after_o:after_o + NT * 256]

    def sem(name):
        return nc.alloc_semaphore(name)

    slot_full = [sem(f"slot_full{i}") for i in range(RING)]
    x_in_s, cst_in, c_in_s, prm_in, row_in, wsm_in, rpb_ld = (sem(n) for n in ("x_in_s", "cst_in", "c_in_s", "prm_in", "row_in", "wsm_in", "rpb_ld"))
    dense_done = sem("dense_done")
    dense_free = [sem("dense_free0"), sem("dense_free1")]
    ada_done, mod_ready, scv_ready = sem("ada_done"), sem("mod_ready"), sem("scv_ready")
    sq_ready, nsum_ready, nrs_ready, h_ready, x_ready = (sem(n) for n in ("sq_ready", "nsum_ready", "nrs_ready", "h_ready", "x_ready"))
    sm_done, cum_done, exx_ready, decay_ready = (sem(n) for n in ("sm_done", "cum_done", "exx_ready", "decay_ready"))
    sm_act, sm_dve = sem("sm_act"), sem("sm_dve")
    na_sq, na_ss, na_rs, na_qk, na_vt, na_vc, na_bias = (sem(n) for n in ("na_sq", "na_ss", "na_rs", "na_qk", "na_vt", "na_vc", "na_bias"))
    na_S, na_max, na_P, na_T, na_PT, na_PV, na_O, na_OT, na_YA = (sem(n) for n in ("na_S", "na_max", "na_P", "na_T", "na_PT", "na_PV", "na_O", "na_OT", "na_YA"))
    conv_done, silu_done, pads_ready = sem("conv_done"), sem("silu_done"), sem("pads_ready")
    dq_sq, dq_ss, dq_rs, dq_n, dq_rot, dq_rope = (sem(n) for n in ("dq_sq", "dq_ss", "dq_rs", "dq_n", "dq_rot", "dq_rope"))
    tr_done, tr_copied = sem("tr_done"), sem("tr_copied")
    dn_ss, dn_rs, dn_on, dn_ot, dn_y = (sem(n) for n in ("dn_ss", "dn_rs", "dn_on", "dn_ot", "dn_y"))
    ss_ot, ss_yz, ss_sq, ss_sum, ss_rs, ss_y = (sem(n) for n in ("ss_ot", "ss_yz", "ss_sq", "ss_sum", "ss_rs", "ss_y"))
    hid_relu, hid_ready, m_ready, out_done = sem("hid_relu"), sem("hid_ready"), sem("m_ready"), sem("out_done")
    eps_ready, bada_in, cst2_in = sem("eps_ready"), sem("bada_in"), sem("cst2_in")
    act_chain, dve_chain, pool_chain = sem("act_chain"), sem("dve_chain"), sem("pool_chain")

    LV = range(1, 7)
    pe_n = ["GK", "GQ", "T0"]
    dve_n = ["MT", "XT1", "AT"]
    act_n = ["X1"]
    for l in LV:
        pe_n += [f"Y{l}", f"Z{l}"] + ([f"T{l}"] if l < 6 else [])
        dve_n += [f"Y{l}", f"X{l}"]
        if l < 6:
            act_n += [f"XT{l}"]
    pe_n += ["WT", "V", "OI", "OA", "ST"]
    dve_n += ["VN", "O", "S"]
    act_n += ["WT"]
    dpe = [Steps(sem(f"dn_pe{d}"), pe_n) for d in range(2)]
    ddve = [Steps(sem(f"dn_dve{d}"), dve_n) for d in range(2)]
    dact = [Steps(sem(f"dn_act{d}"), act_n) for d in range(2)]
    dpool = [Steps(sem(f"dn_pool{d}"), ["KE", "KD"]) for d in range(2)]
    dpre = [Steps(sem(f"dn_pre{d}"), ["R", "DM", "DA"]) for d in range(2)]
    dn_seg, dn_exp = [sem(f"dn_seg{d}") for d in range(2)], [sem(f"dn_exp{d}") for d in range(2)]
    spe = [Steps(sem(f"ss_pe{d}"), ["SEG0", "CB", "SEG1", "Y0", "Y1", "INT", "ST"]) for d in range(2)]
    sdve = [Steps(sem(f"ss_dve{d}"), ["CBM", "XD", "W0", "W1", "YA", "H"]) for d in range(2)]
    sact = [Steps(sem(f"ss_act{d}"), ["D0", "D1"]) for d in range(2)]
    spool = [Steps(sem(f"ss_pool{d}"), ["R0", "R1", "XW"]) for d in range(2)]

    TILES = ((0, 1, 2, 3, 4, 5), (1, 0, 5, 4, 3, 2))

    def changed(a, l, d):
        return a.rearrange("p (a two s) -> p a two s", two=2, s=1 << l)[:, :, d]

    def halves(a, l, d):
        return a.rearrange("p h (a two s) -> p h a two s", two=2, s=1 << l)[:, :, :, d]

    def packed(a, l):
        return a.rearrange("p (h a s) -> p h a s", h=4, s=1 << l)

    def first_visit(n):
        return n in (0, 2, 3)

    def job(layer, stage, i):
        return layer * NJOB + JOB_AT[stage] + i

    def segs_of(layer):
        return SEGS if layer < DEPTH - 1 else SEGS[:1]

    def out_tiles(layer, sg):
        def first(l):
            return 0 if l < DEPTH - 1 else CTX // P

        return first(layer), sum(2 * (NT - first(l)) for l in range(layer)) + sg * (NT - first(layer))

    def na_blocks(layer):
        return ([(False, 0), (False, 1)] if layer < DEPTH - 1 else []) + [(True, b) for b in range(4)]

    def flat(a):
        return a.rearrange("p a b -> p (a b)")

    def na_u0(layer, gi):
        return sum(2 * 4 * len(na_blocks(l)) for l in range(layer)) + gi * 4 * len(na_blocks(layer))

    def counted(j):
        r = j % NJOB
        return not (JOB_AT["out"] <= r < JOB_AT["ff1"] or r >= JOB_AT["ff2"])

    def free_count(j):
        return sum(counted(i) for i in range(j % 2, j + 1, 2))

    def bcast(a, n):
        return a.unsqueeze(2).to_broadcast([a.shape[0], a.shape[1], n])

    def over(a, h):
        return a.unsqueeze(1).to_broadcast([a.shape[0], h, a.shape[1]])

    def col(layer, name, i=0):
        at = COL_AT[name] + i
        return prm[:, at:at + 1]

    def window(b):
        return min(max(b * BLK_C - 8, 0), GW - 32)

    def nak(a, b):
        return a.rearrange("p (r c) -> p c r", r=GR)[:, window(b):window(b) + 32]

    def by_block(a):
        return a.rearrange("p (b r i) -> p r b i", b=4, r=GR)

    def by_column(a):
        return a.rearrange("p (c r) -> p r c", r=GR)

    def naq_of(a, b):
        return a.rearrange("p (r c) -> p r c", r=GR)[:, :, b * BLK_C:(b + 1) * BLK_C]

    VAR = (0, 1, 1, 2)

    block_ctx = nc.Block()
    with block_ctx as block:

        @block.sync
        def _(sp):
            def released():
                out = [(ada_done, i + 1) for i in range(ADA0)]
                for layer in range(DEPTH):
                    base = layer * NJOB
                    for st in ("na0", "na1", "dn0", "dn1", "ss0", "ss1"):
                        out += [(dense_done, base + JOB_AT[st] + 2 * i + 2) for i in range(PANELS[st])]
                    for m in range(4):
                        for i, e in enumerate((2, 4, 6, 10, 12)):
                            out.append((dense_done, base + JOB_AT["merge"] + 12 * m + e))
                            if layer == 0 and m and i != 3:
                                out.append((ada_done, ADA0 + 4 * (m - 1) + min(i, 3) + 1))
                    for st, jobs, at in (("out", 2, ADA_OUT), ("ff1", 2, ADA_P), ("ff2", 1, ADA_P + 16)):
                        for i in range(JOBS[st] // jobs):
                            done = (dense_done, base + JOB_AT[st] + jobs * (i + 1))
                            out += [done] * (2 if st == "ff2" else 1)
                            if layer == 0:
                                out.append((ada_done, at + i + 1))
                return out

            uses = released()
            sp.dma_start(cst[:, 0:P * len(SQ)], const_in[:, 0:P * len(SQ)]).then_inc(cst_in, 16)
            sp.dma_start(X[:, :, :], x_in).then_inc(x_in_s, 16)
            for n in range(DEPTH * NPANEL):
                if n >= RING:
                    s, v = uses[n - RING]
                    sp.wait_ge(s, v)
                sp.dma_start(ring[:, n % RING * PANEL:(n % RING + 1) * PANEL], stream[n]).then_inc(slot_full[n % RING], 16)
            for k in range(KC):
                sp.wait_ge(x_ready, 2 * KC * DEPTH - KC + k + 1)
                sp.dma_start(out[:, k, :], X[:, k, CTX:]).then_inc(out_done, 16)
            sp.wait_ge(out_done, 16 * KC)

        @block.gpsimd
        def _(pool):
            chain = [0]

            def link(ins):
                chain[0] += 1
                ins.then_inc(pool_chain, 1)
                pool.wait_ge(pool_chain, chain[0])

            g = nc.gpsimd
            g.dma_start(cvec, c_in).then_inc(c_in_s, 16)
            g.dma_start(bada[:, :], bada_in_).then_inc(bada_in, 16)
            for layer in range(DEPTH):
                if layer:
                    pool.wait_ge(h_ready, 2 * layer)
                g.dma_start(prm[:, :], cols_in[layer]).then_inc(prm_in, 16)
                g.dma_start(rowp[:, :], rows_in[layer].partition_broadcast(P)).then_inc(row_in, 16)
                g.dma_start(wsm, wsmall_in[layer]).then_inc(wsm_in, 16)
                for gi in range(2):
                    G = 2 * layer + gi
                    pool.wait_ge(h_ready, 2 * layer + 1)
                    if G == 0:
                        g.dma_start(cst[:, P * len(SQ):], const_in[:, P * len(SQ):]).then_inc(cst2_in, 16)
                    if gi:
                        pool.wait_ge(na_bias, G)
                    for r in range(GR):
                        src = rpb_in[layer, 4 * gi:4 * gi + 4, :, GR - 1 - r:2 * GR - 1 - r, :]
                        g.dma_start(nag[r * BLK_C:(r + 1) * BLK_C], src.rearrange("h i r m -> i h r m")).then_inc(rpb_ld, 16)
                    pool.wait_ge(rpb_ld, 16 * GR * (G + 1))
                    pool.wait_ge(cst2_in, 16)
                    if gi == 1:
                        pool.wait_ge(na_max, na_u0(layer, 1))
                    for h in range(4):
                        for v, m0 in enumerate((16, 8, 0)):
                            ins = g.tensor_tensor(nab[:, h, v].rearrange("p (c r) -> p r c", r=GR), nag[:, h, :, m0:m0 + 32],
                                                  nam[:, v].rearrange("p (r c) -> p r c", r=GR), ALU.add)
                    ins.then_inc(na_bias, 1)
                for hg in range(2):
                    G = 2 * layer + hg
                    pool.wait_ge(tr_copied, 6 * (4 * layer + hg + 1))

                    def decay_masks(n):
                        s = 6 * G + n
                        for d in range(2):
                            c0 = dec_col("dn", d, 4 * hg)
                            g.tensor_tensor(dR[d], over((C["le"], C["ge"])[d], 4), bcast(dec[:, TILES[d][n], c0:c0 + 4], P),
                                            ALU.mult).then_inc(dpre[d].sem, 1)
                        for d in range(2):
                            t = TILES[d][n]
                            pool.wait_ge(dn_exp[d], s + 1)
                            link(g.tensor_tensor(dDM[d], dD[d], over((C["lt"], C["gt"])[d], 4), ALU.mult))
                            g.tensor_tensor(dDM[d], dDM[d], bcast(beta[:, t, 8 * d + 4 * hg:8 * d + 4 * hg + 4], P), ALU.mult).then_inc(dpre[d].sem, 1)
                            g.tensor_tensor(dDA[d], dD[d], over((C["le"], C["ge"])[d], 4), ALU.mult).then_inc(dpre[d].sem, 1)

                    for n in range(6):
                        s = 6 * G + n
                        if s:
                            for d in range(2):
                                pool.wait_ge(dpe[d].sem, dpe[d].at(s - 1, "ST"))
                        if n == 0:
                            decay_masks(0)
                        for d in range(2):
                            t = TILES[d][n]
                            c0 = dec_col("dn", d, 4 * hg)
                            kk = kvt[:, t, 0:256].rearrange("p (h x) -> p h x", h=4)
                            g.tensor_tensor(dKE[d], kk, bcast(EXX[:, t, 0, c0:c0 + 4], 64), ALU.mult).then_inc(dpool[d].sem, 1)
                            g.tensor_tensor(dKD[d], kk, bcast(EXX[:, t, 1, c0:c0 + 4], 64), ALU.mult).then_inc(dpool[d].sem, 1)
                        if n < 5:
                            decay_masks(n + 1)
                for sg in range(2):
                    G = 2 * layer + sg
                    pool.wait_ge(tr_copied, 6 * (4 * layer + 2 + sg + 1))
                    for n in range(6):
                        s = 6 * G + n
                        for d in range(2):
                            t = TILES[d][n]
                            if s:
                                pool.wait_ge(spe[d].sem, spe[d].at(s - 1, "ST"))
                            for half in range(2):
                                if half:
                                    pool.wait_ge(spe[d].sem, spe[d].at(s, "SEG0"))
                                c0 = dec_col("ss", d, 8 * sg + 4 * half)
                                g.tensor_tensor(sR[d].rearrange("p (h x) -> p h x", h=4), over((C["le"], C["ge"])[d], 4),
                                                bcast(dec[:, t, c0:c0 + 4], P), ALU.mult).then_inc(spool[d].sem, 1)
                        for d in range(2):
                            t = TILES[d][n]
                            c0 = dec_col("ss", d, 8 * sg)
                            pool.wait_ge(spe[d].sem, spe[d].at(s, "SEG1"))
                            pool.wait_ge(sdve[d].sem, sdve[d].at(s, "XD"))
                            g.tensor_tensor(sR[d].rearrange("p (h x) -> p h x", h=8), sXD[d].rearrange("p (h x) -> p h x", h=8),
                                            bcast(EXX[:, t, 1, c0:c0 + 8], 64), ALU.mult).then_inc(spool[d].sem, 1)

        @block.scalar
        def _(act):
            chain = [0]
            a = nc.scalar

            def link(ins):
                chain[0] += 1
                ins.then_inc(act_chain, 1)
                act.wait_ge(act_chain, chain[0])

            def rsqrt(out_ap, in_aps, out_parts, scale, last_sem, extra=0.0):
                for o, i in zip(out_parts, in_aps):
                    ins = a.activation(o, i, ACT.Ln, scale=scale, bias=eps_t[:, 0:1])
                link(ins)
                a.activation(out_ap, out_ap, ACT.Exp, scale=-0.5, bias=(extra_t[:, 0:1] if extra else 0.0)).then_inc(last_sem, 1)

            def norm(q, segs):
                layer = q // 2
                if q == 0:
                    act.wait_ge(x_in_s, 16)
                for k in range(KC):
                    if q:
                        act.wait_ge(x_ready, KC * (q - 1) + k + 1)
                    if q and k == 0:
                        act.wait_ge(x_ready, KC * q)
                    if k >= 2:
                        act.wait_ge(nsum_ready, KC * q + k - 1)
                    lo, hi = (0, T) if len(segs) == 2 else (CTX, T)
                    a.activation(nsq[:, k % 2, lo:hi], X[:, k, lo:hi], ACT.Square).then_inc(sq_ready, 1)
                act.wait_ge(nsum_ready, KC * (q + 1))
                rsqrt(nrs[:, lo:hi], [ps[4 + i][:, 0:w] for i, (o, w) in enumerate(segs)], [nrs[:, o:o + w] for o, w in segs],
                      1.0 / D, nrs_ready)

            def evac(j, outs, func=ACT.Copy, segs=SEGS):
                act.wait_ge(dense_done, j + 1)
                for i, (o, w) in enumerate(segs):
                    ins = a.activation(outs[i], ps[2 * (j % 2) + i][:, 0:w], func)
                return ins

            def group_proj(layer, stage, gq, raw_b, cv_b, dests, zj, z_dest, bias_cols, after=None):
                act.wait_ge(pads_ready, gq + 1)
                for c in range(7):
                    if c < 6:
                        if c >= 2:
                            act.wait_ge(conv_done, 6 * gq + c - 1)
                        j = job(layer, stage, c)
                        evac(j, [raw_b[:, c % 2, RAW0[1]:RAW0[1] + LAT], raw_b[:, c % 2, 2:2 + CTX]]).then_inc(dense_free[j % 2], 1)
                    if c >= 1:
                        act.wait_ge(conv_done, 6 * gq + c)
                        for o, w, r0 in ((CTX, LAT, RAW0[1]), (0, CTX, 2)):
                            b = prm[:, bias_cols + c - 1:bias_cols + c] if bias_cols is not None else 0.0
                            ins = a.activation(dests[c - 1][:, o:o + w], cv_b[:, (c - 1) % 2, r0:r0 + w], ACT.Silu, bias=b)
                        ins.then_inc(silu_done, 1)
                    if after:
                        after(c)
                for c in range(zj):
                    j = job(layer, stage, 6 + c)
                    evac(j, [z_dest[:, c, o:o + w] for o, w in segs_of(layer)], ACT.Silu, segs_of(layer)).then_inc(dense_free[j % 2], 1)

            act.wait_ge(c_in_s, 16)
            act.wait_ge(eps_ready, 2)
            a.activation(scv, cvec, ACT.Silu).then_inc(scv_ready, 1)
            for layer in range(DEPTH):
                segs = segs_of(layer)
                norm(2 * layer, SEGS)
                act.wait_ge(row_in, 16 * (layer + 1))
                link(a.activation(rowp[:, NDEC:], rowp[:, NDEC:], ACT.Exp))
                act.wait_ge(sm_done, layer + 1)
                smp = ps[6][:, 0:NT * NSM].rearrange("p (t c) -> p t c", t=NT)
                a.activation(beta, smp[:, :, 0:16], ACT.Exp, scale=-1.0).then_inc(sm_act, 1)
                act.wait_ge(sm_dve, 2 * layer + 1)
                link(a.activation(spl, dec, ACT.Abs))
                link(a.activation(spl, spl, ACT.Exp, scale=-1.0))
                a.activation(spl, spl, ACT.Ln, bias=1.0).then_inc(sm_act, 1)
                act.wait_ge(cum_done, layer + 1)
                for i in range(2):
                    ins = a.activation(EXX[:, 3 * i:3 * i + 3].rearrange("p t e c -> p (t e c)"), ps[4 + i][:, 0:9 * NDEC], ACT.Exp)
                ins.then_inc(exx_ready, 1)
                blocks = na_blocks(layer)
                units = [(b, h) for b in range(len(blocks)) for h in range(4)]
                for gi in range(2):
                    G = 2 * layer + gi
                    for c in range(6):
                        j = job(layer, f"na{gi}", c)
                        dst = naq[:, c] if c < 4 else nav[:, c - 4]
                        act.wait_ge(dense_done, j + 1)
                        lat = ps[2 * (j % 2)]
                        if c < 2:
                            a.activation(by_block(dst[:, CTX:]), lat.rearrange("p (r b i) -> p r b i", b=4, r=GR), ACT.Copy)
                        elif c < 4:
                            a.activation(dst[:, CTX:], lat, ACT.Copy)
                        else:
                            a.activation(by_column(dst[:, CTX:]), lat.rearrange("p (r c) -> p r c", r=GR), ACT.Copy)
                        a.activation(dst[:, 0:CTX], ps[2 * (j % 2) + 1][:, 0:CTX], ACT.Copy).then_inc(dense_free[j % 2], 1)
                        if c < 4:
                            if c >= 2:
                                act.wait_ge(na_ss, 4 * G + c - 1)
                            act.wait_ge(dense_free[j % 2], free_count(j))
                            a.activation(nasq[:, c % 2], dst, ACT.Square).then_inc(na_sq, 1)
                        if 1 <= c <= 4:
                            cc = c - 1
                            act.wait_ge(na_ss, 4 * G + cc + 1)
                            if cc >= 2:
                                act.wait_ge(na_qk, 4 * G + cc - 1)
                            rsqrt(nars[:, cc % 2], [ps[4 + 2 * (cc % 2) + i][:, 0:w] for i, (o, w) in enumerate(SEGS)],
                                  [nars[:, cc % 2, o:o + w] for o, w in SEGS], 1.0 / HD, na_rs)
                    for i in range(5):
                        act.wait_ge(na_vt, 5 * G + i + 1)
                        a.activation(navt[:, 2 * i:2 * i + 2].rearrange("p t c -> p (t c)"), ps[4 + i % 4], ACT.Copy).then_inc(na_vc, 1)
                    u0 = na_u0(layer, gi)
                    b0 = u0 // 4

                    def probs(u):
                        lat = blocks[units[u][0]][0]
                        act.wait_ge(na_max, u0 + u + 1)
                        lo = 0 if lat else 256
                        if u >= 2:
                            act.wait_ge(na_T, u0 + u - 1)
                        hcol = units[u][0] % 2 * 4 + units[u][1]
                        a.activation(naP[:, u % 2, lo:512], na_sbank[u % 3][:, lo:512], ACT.Exp, bias=nast[:, 0, u % 2:u % 2 + 1],
                                     accum_out=nast[:, 1, hcol:hcol + 1]).then_inc(na_P, 1)

                    def ya(b):
                        lat, i = blocks[b]
                        act.wait_ge(na_OT, b0 + b + 1)
                        for c in range(2):
                            src = na_tbank[:, c * P:(c + 1) * P]
                            if lat:
                                dst = naq_of(YA[:, 2 * gi + c, CTX:], i)
                                ins = a.activation(dst, src.rearrange("p (r c) -> p r c", r=GR), ACT.Copy)
                            else:
                                ins = a.activation(YA[:, 2 * gi + c, i * P:(i + 1) * P], src, ACT.Copy)
                        ins.then_inc(na_YA, 1)

                    probs(0)
                    for u in range(len(units)):
                        if u + 1 < len(units):
                            probs(u + 1)
                        lo = 0 if blocks[units[u][0]][0] else 256
                        act.wait_ge(na_T, u0 + u + 1)
                        if u >= 2:
                            act.wait_ge(na_PV, u0 + u - 1)
                        a.activation(naPT[:, u % 2, lo:512], ps[6][:, lo:512], ACT.Copy).then_inc(na_PT, 1)
                        if units[u][1] == 3 and units[u][0] > 0:
                            ya(units[u][0] - 1)
                    ya(len(blocks) - 1)
                for hg in range(2):
                    G = 2 * layer + hg
                    gq = 4 * layer + hg

                    def l2_norm(c):
                        if 0 <= c - 1 < 4:
                            act.wait_ge(silu_done, 6 * gq + c)
                            a.activation(sqb[:, (c - 1) % 2], QK[:, c - 1], ACT.Square).then_inc(dq_sq, 1)
                        x = c - 2
                        if 0 <= x < 4:
                            act.wait_ge(dq_ss, 4 * G + x + 1)
                            if x >= 3:
                                act.wait_ge(dq_rope, 4 * G + x - 2)
                            rsqrt(rsb[:, x % 3], [ps[4 + i][:, 0:w] for i, (o, w) in enumerate(SEGS)],
                                  [rsb[:, x % 3, o:o + w] for o, w in SEGS], 1.0, dq_rs, extra=(1.0 if x < 2 else 0.0))

                    group_proj(layer, f"dn{hg}", gq, rawp, cv, [QK[:, 0], QK[:, 1], QK[:, 2], QK[:, 3], dnV[:, 0], dnV[:, 1]], 2, zb, None,
                               l2_norm)
                    for t in range(NT):
                        act.wait_ge(tr_done, 6 * gq + t + 1)
                        a.activation(kvt[:, t], ps[4 + t % 4], ACT.Copy).then_inc(tr_copied, 1)

                    def exp_decays(s):
                        for d in range(2):
                            act.wait_ge(dn_seg[d], s + 1)
                            if s:
                                act.wait_ge(ddve[d].sem, ddve[d].at(s - 1, "AT"))
                            a.activation(flat(dD[d]), ps[4 * d + 3], ACT.Exp).then_inc(dn_exp[d], 1)

                    exp_decays(6 * G)
                    for n in range(6):
                        s = 6 * G + n
                        for d in range(2):
                            act.wait_ge(dpe[d].sem, dpe[d].at(s, "T0"))
                            a.activation(flat(dX[d]), ps[4 * d], ACT.Copy).then_inc(dact[d].sem, 1)
                        for l in range(1, 6):
                            for d in range(2):
                                act.wait_ge(dpe[d].sem, dpe[d].at(s, f"T{l}"))
                                a.activation(flat(dXT[d]), ps[4 * d + 2], ACT.Copy).then_inc(dact[d].sem, 1)
                            if l == 3 and n < 5:
                                exp_decays(s + 1)
                        for d in range(2):
                            act.wait_ge(dpe[d].sem, dpe[d].at(s, "WT"))
                            a.activation(flat(dWT[d]), ps[4 * d][:, 0:256], ACT.Copy, scale=-1.0).then_inc(dact[d].sem, 1)
                    act.wait_ge(dn_ss, G + 1)
                    rsqrt(smt[:, 0:24], [smt[:, 0:24]], [smt[:, 0:24]], 1.0 / HD, dn_rs)
                for sg in range(2):
                    G = 2 * layer + sg
                    gq = 4 * layer + 2 + sg
                    group_proj(layer, f"ss{sg}", gq, srawp, scvb,
                               [YC[:, 4 * sg + c] for c in range(4)] + [BC[:, 0], BC[:, 1]], 0, None, COL_AT["sscb"] + 6 * sg)
                    for t in range(NT):
                        act.wait_ge(tr_done, 6 * gq + t + 1)
                        a.activation(xt[:, t], ps[4 + t % 2], ACT.Copy)
                        a.activation(bt[:, t], ps[6 + t % 2][:, 0:P], ACT.Copy).then_inc(tr_copied, 1)
                    for n in range(6):
                        s = 6 * G + n
                        for half in range(2):
                            for d in range(2):
                                act.wait_ge(spe[d].sem, spe[d].at(s, f"SEG{half}"))
                                if half:
                                    act.wait_ge(spe[d].sem, spe[d].at(s, "Y0"))
                                elif s:
                                    act.wait_ge(spe[d].sem, spe[d].at(s - 1, "Y1"))
                                a.activation(sW[d], ps[4 * d + half], ACT.Exp).then_inc(sact[d].sem, 1)
                    for d in range(2):
                        act.wait_ge(sdve[d].sem, sdve[d].at(6 * G + 5, "H"))
                    for c in range(4):
                        j = job(layer, f"ss{sg}", 6 + c)
                        evac(j, [szb[:, c, o:o + w] for o, w in segs], ACT.Silu, segs).then_inc(dense_free[j % 2], 1)
                    t0, ot0 = out_tiles(layer, sg)
                    act.wait_ge(ss_yz, ot0 + NT - t0)
                    act.wait_ge(ss_ot, ot0 + NT - t0)
                    for c in range(4):
                        a.activation(ssq[:, c, t0 * P:], YC[:, 4 * sg + c, t0 * P:], ACT.Square).then_inc(ss_sq, 1)
                    act.wait_ge(ss_sum, G + 1)
                    rsqrt(srs[:, t0 * P:], [ps[4 + i][:, 0:w] for i, (o, w) in enumerate(segs)], [srs[:, o:o + w] for o, w in segs], 1.0 / 512, ss_rs)
                act.wait_ge(ss_y, 2 * (layer + 1))
                for m in range(4):
                    for i in range(6):
                        j = job(layer, "merge", 12 * m + i)
                        if m:
                            act.wait_ge(m_ready, KC * layer + 2 * m)
                        evac(j, [gates[:, i, o:o + w] for o, w in segs], ACT.Sigmoid, segs).then_inc(dense_free[j % 2], 1)
                norm(2 * layer + 1, segs)
                for c in range(FF // P):
                    if c == 0:
                        act.wait_ge(h_ready, 2 * layer + 2)
                    j = job(layer, "ff1", c)
                    evac(j, [hid[:, c, o:o + w] for o, w in segs], ACT.Relu, segs).then_inc(dense_free[j % 2], 1)

        @block.vector
        def _(dve):
            chain = [0]
            v = nc.vector

            def link(ins):
                chain[0] += 1
                ins.then_inc(dve_chain, 1)
                dve.wait_ge(dve_chain, chain[0])

            dve.wait_ge(cst_in, 16)
            v.memset(eps_t[:, :], EPS).then_inc(eps_ready, 1)
            v.memset(extra_t[:, :], -math.log(8.0)).then_inc(eps_ready, 1)

            def modulation(layer, lo, hi, bank, done):
                dve.wait_ge(ada_done, done)
                dve.wait_ge(bada_in, 16)
                at = 48 * layer
                v.tensor_tensor(mods[layer][:, lo:hi], bank[:, 0:2 * (hi - lo)].rearrange("p (f s) -> p f s", s=2),
                                bcast(bada[:, at + lo:at + hi], 2), ALU.add).then_inc(mod_ready, 1)

            def norm(q, segs, part):
                mod = mods[q // 2]
                layer = q // 2
                if q:
                    dve.wait_ge(h_ready, q)
                gain = prm[:, COL_AT["n1"] + 8 * part:COL_AT["n1"] + 8 * part + 8]
                link(v.scalar_tensor_tensor(out=am, in0=mod[:, 24 * part + 8:24 * part + 16], scalar=1.0, in1=bcast(gain, 2),
                                            op0=ALU.add, op1=ALU.mult))
                dve.wait_ge(nrs_ready, q + 1)
                lo, hi = (0, T) if len(segs) == 2 else (CTX, T)
                for k in range(KC):
                    link(v.tensor_tensor(H[:, k, lo:hi], X[:, k, lo:hi], nrs[:, lo:hi], ALU.mult))
                    for i, (o, w) in enumerate(segs):
                        ins = v.tensor_scalar(H[:, k, o:o + w], H[:, k, o:o + w], am[:, k, i:i + 1], mod[:, 24 * part + k, i:i + 1], ALU.mult, ALU.add)
                ins.then_inc(h_ready, 1)

            def convs(layer, gq, raw_b, cv_b, taps, after=None):
                for b in range(2):
                    ins = v.memset(raw_b[:, b], 0.0)
                ins.then_inc(pads_ready, 1)
                st = "dn" if gq % 4 < 2 else "ss"
                for c in range(6):
                    j = job(layer, f"{st}{gq % 2}", c)
                    dve.wait_ge(dense_free[j % 2], free_count(j))
                    if c >= 2:
                        dve.wait_ge(silu_done, 6 * gq + c - 1)
                    o = cv_b[:, c % 2, 2:RAWW - 2]
                    tap = [prm[:, taps + 5 * c + k:taps + 5 * c + k + 1] for k in range(5)]
                    link(v.tensor_scalar(o, raw_b[:, c % 2, 2:RAWW - 2], tap[2], None, ALU.mult))
                    for k in (0, 1, 3, 4):
                        ins = v.scalar_tensor_tensor(out=o, in0=raw_b[:, c % 2, k:k + T + 2], scalar=tap[k], in1=o, op0=ALU.mult, op1=ALU.add)
                        if k < 4:
                            link(ins)
                    ins.then_inc(conv_done, 1)
                    if after:
                        after(c)

            for layer in range(DEPTH):
                segs = segs_of(layer)
                if layer == 0:
                    modulation(0, 0, 2 * ADA0, ada_bank, ADA0)
                    dve.wait_ge(mod_ready, 1)
                mod = mods[layer]
                dve.wait_ge(prm_in, 16 * (layer + 1))
                norm(2 * layer, SEGS, 0)
                link(v.tensor_scalar(qg8[:, :], col(layer, "qg"), HD ** -0.5, None, ALU.mult))
                dve.wait_ge(row_in, 16 * (layer + 1))
                dve.wait_ge(sm_act, 2 * layer + 1)
                smp = ps[6][:, 0:NT * NSM].rearrange("p (t c) -> p t c", t=NT)
                v.tensor_tensor(dec, smp[:, :, 16:NSM], rowp[:, 0:NDEC].unsqueeze(1).to_broadcast([P, NT, NDEC]), ALU.add).then_inc(sm_dve, 1)
                link(v.tensor_scalar(beta, beta, 1.0, None, ALU.add))
                link(v.reciprocal(beta, beta))
                dve.wait_ge(sm_act, 2 * layer + 2)
                link(v.scalar_tensor_tensor(out=spl, in0=dec, scalar=0.0, in1=spl, op0=ALU.max, op1=ALU.add))
                v.scalar_tensor_tensor(out=dec, in0=spl, scalar=-1.0, in1=rowp[:, NDEC:].unsqueeze(1).to_broadcast([P, NT, NDEC]),
                                       op0=ALU.mult, op1=ALU.mult).then_inc(sm_dve, 1)
                blocks = na_blocks(layer)
                units = [(b, h) for b in range(len(blocks)) for h in range(4)]
                for gi in range(2):
                    G = 2 * layer + gi
                    for c in range(4):
                        dve.wait_ge(na_rs, 4 * G + c + 1)
                        gain = qg8[:, 0:1] if c < 2 else col(layer, "kg")
                        v.scalar_tensor_tensor(out=naq[:, c], in0=naq[:, c], scalar=gain, in1=nars[:, c % 2], op0=ALU.mult, op1=ALU.mult).then_inc(na_qk, 1)
                    u0 = na_u0(layer, gi)
                    b0 = u0 // 4
                    dve.wait_ge(na_bias, G + 1)

                    def outp(b):
                        dve.wait_ge(na_PV, u0 + 4 * b + 4)
                        hc = b % 2 * 4
                        link(v.reciprocal(nast[:, 2, 0:4], nast[:, 1, hc:hc + 4]))
                        v.tensor_tensor(naO[:, b % 2].rearrange("p (h x) -> p h x", h=4),
                                        na_obank[b % 2][:, 0:256].rearrange("p (h x) -> p h x", h=4),
                                        bcast(nast[:, 2, 0:4], 64), ALU.mult).then_inc(na_O, 1)

                    for u, (b, h) in enumerate(units):
                        lat, i = blocks[b]
                        dve.wait_ge(na_S, u0 + u + 1)
                        sp_ = na_sbank[u % 3]
                        lo = 256
                        if lat:
                            link(v.tensor_tensor(sp_[:, 0:256], sp_[:, 0:256], nab[:, h, VAR[i]], ALU.add))
                            lo = 0
                        link(v.reduce_max(nast[:, 0, 2 + u % 2:3 + u % 2], sp_[:, lo:512], AX.X))
                        if u >= 2:
                            dve.wait_ge(na_P, u0 + u - 1)
                        v.tensor_scalar(nast[:, 0, u % 2:u % 2 + 1], nast[:, 0, 2 + u % 2:3 + u % 2], -1.0, None, ALU.mult).then_inc(na_max, 1)
                        if h == 1 and b > 0:
                            outp(b - 1)
                    outp(len(blocks) - 1)
                for hg in range(2):
                    G = 2 * layer + hg
                    gq = 4 * layer + hg
                    if hg == 0:
                        dve.wait_ge(na_YA, (na_u0(layer, 1) + len(units)) // 4)

                    def norm_rope(c):
                        x = c - 4
                        if x >= 0:
                            q = QK[:, x]
                            dve.wait_ge(dq_rot, 4 * G + x + 1)
                            dve.wait_ge(cst2_in, 16)
                            tmp = rsb[:, x % 3, 0:LAT]
                            link(v.tensor_tensor(tmp, ps[6 + x % 2], sin, ALU.mult))
                            link(v.tensor_tensor(q[:, CTX:], q[:, CTX:], cos, ALU.mult))
                            v.tensor_tensor(q[:, CTX:], q[:, CTX:], tmp, ALU.add).then_inc(dq_rope, 1)
                        x = c - 2
                        if 0 <= x < 4:
                            dve.wait_ge(dq_rs, 4 * G + x + 1)
                            v.tensor_tensor(QK[:, x], QK[:, x], rsb[:, x % 3], ALU.mult).then_inc(dq_n, 1)

                    convs(layer, gq, rawp, cv, COL_AT["dncv"] + 30 * hg, norm_rope)
                    norm_rope(6)
                    norm_rope(7)
                    dve.wait_ge(tr_copied, 6 * (gq + 1))
                    for d in range(2):
                        link(v.memset(dnS[:, d].rearrange("p g v -> p (g v)"), 0.0))
                    for n in range(6):
                        s = 6 * G + n
                        for d in range(2):
                            dve.wait_ge(dpe[d].sem, dpe[d].at(s, "GK"))
                            dve.wait_ge(dpre[d].sem, dpre[d].at(s, "DM"))
                            for e in range(2):
                                ins = v.tensor_tensor(dMT[d][:, e::2], ps[4 * d + e][:, 0:256].rearrange("p (h x) -> p h x", h=2), dDM[d][:, e::2], ALU.mult)
                            ins.then_inc(ddve[d].sem, 1)
                            dve.wait_ge(ddve[d].sem, ddve[d].at(s, "MT"))
                            link(v.tensor_tensor(dXT[d], dMT[d], over(C[("um0", "lm0")[d]], 4), ALU.mult))
                            v.tensor_tensor(dXT[d], over(C["ident"], 4), dXT[d], ALU.subtract).then_inc(ddve[d].sem, 1)
                        for d in range(2):
                            dve.wait_ge(dpe[d].sem, dpe[d].at(s, "GQ"))
                            dve.wait_ge(dpre[d].sem, dpre[d].at(s, "DA"))
                            for e in range(2):
                                ins = v.tensor_tensor(dAT[d][:, e::2], ps[4 * d + 2 + e][:, 0:256].rearrange("p (h x) -> p h x", h=2), dDA[d][:, e::2], ALU.mult)
                            ins.then_inc(ddve[d].sem, 1)
                        for l in LV:
                            for d in range(2):
                                dve.wait_ge(dpe[d].sem, dpe[d].at(s, f"Y{l}"))
                                mask = changed(C[f"{'lu'[d]}m{l}"], l, d).unsqueeze(1).to_broadcast([P, 4, 64 >> l, 1 << l])
                                v.tensor_tensor(packed(flat(dY[d])[:, 0:256], l), halves(ps[4 * d].rearrange("p (h x) -> p h x", h=4), l, d), mask, ALU.mult).then_inc(ddve[d].sem, 1)
                            for d in range(2):
                                dve.wait_ge(dpe[d].sem, dpe[d].at(s, f"Z{l}"))
                                z = ps[4 * d + 1][:, 0:256]
                                if l < 6:
                                    x = halves(dX[d], l, d)
                                    ins = v.tensor_tensor(x, x, packed(z, l), ALU.subtract)
                                else:
                                    o = slice(64 * d, 64 * d + 64)
                                    x = dXT[d][o, :, 64 * (1 - d):64 * (1 - d) + 64]
                                    ins = v.tensor_tensor(x, x, z[o].rearrange("p (h x) -> p h x", h=4), ALU.subtract)
                                ins.then_inc(ddve[d].sem, 1)
                        for d in range(2):
                            t = TILES[d][n]
                            bc = 8 * d + 4 * hg
                            dve.wait_ge(dpe[d].sem, dpe[d].at(s, "V"))
                            v.tensor_tensor(dVN[d], ps[4 * d + 1][:, 0:256].rearrange("p (h x) -> p h x", h=4),
                                            bcast(beta[:, t, bc:bc + 4], 64), ALU.mult).then_inc(ddve[d].sem, 1)
                        for d in range(2):
                            t = TILES[d][n]
                            c0 = dec_col("dn", d, 4 * hg)
                            dve.wait_ge(dpe[d].sem, dpe[d].at(s, "ST"))
                            o = dno[:, t].rearrange("p (h x) -> p h x", h=4)
                            tmp = o if first_visit(n) else dTmp[d]
                            link(v.tensor_tensor(tmp, ps[4 * d + 2][:, 0:256].rearrange("p (h x) -> p h x", h=4),
                                                 bcast(EXX[:, t, 0, c0:c0 + 4], 64), ALU.mult))
                            if not first_visit(n):
                                link(v.tensor_tensor(o, o, tmp, ALU.add))
                            v.tensor_tensor(dno[:, t], dno[:, t], ps[4 * d + 3][:, 0:256], ALU.add).then_inc(ddve[d].sem, 1)
                            for h in range(4):
                                sl = slice(64 * (h % 2), 64 * (h % 2) + 64)
                                st = dnS[sl, d, h // 2, sl]
                                ins = v.scalar_tensor_tensor(out=st, in0=st, scalar=EXX[sl, t, 2, c0 + h:c0 + h + 1],
                                                             in1=ps[4 * d + 3][sl, 256 + h * 64:256 + h * 64 + 64], op0=ALU.mult, op1=ALU.add)
                            ins.then_inc(ddve[d].sem, 1)
                    dve.wait_ge(ddve[1].sem, ddve[1].at(6 * G + 5, "O"))
                    dve.wait_ge(ddve[0].sem, ddve[0].at(6 * G + 5, "O"))
                    of = dno.rearrange("p t c -> p (t c)")
                    link(v.tensor_tensor(dn_scr, of, of, ALU.mult))
                    v.reduce_sum(smt[:, 0:24], dn_scr.rearrange("p (g x) -> p g x", x=64), AX.X).then_inc(dn_ss, 1)
                    dve.wait_ge(dn_rs, G + 1)
                    v.tensor_tensor(of.rearrange("p (g x) -> p g x", x=64), of.rearrange("p (g x) -> p g x", x=64),
                                    bcast(smt[:, 0:24], 64), ALU.mult).then_inc(dn_on, 1)
                    dve.wait_ge(dn_ot, G + 1)
                    for c in range(2):
                        for i, (o, w) in enumerate(segs):
                            ins = v.scalar_tensor_tensor(out=YB[:, 2 * hg + c, o:o + w], in0=ps[4 + 2 * c + i][:, 0:w], scalar=col(layer, "dng"),
                                                         in1=zb[:, c, o:o + w], op0=ALU.mult, op1=ALU.mult)
                    ins.then_inc(dn_y, 1)
                for sg in range(2):
                    G = 2 * layer + sg
                    gq = 4 * layer + 2 + sg
                    convs(layer, gq, srawp, scvb, COL_AT["sscv"] + 30 * sg)
                    dve.wait_ge(tr_copied, 6 * (gq + 1))
                    link(v.memset(ssH.rearrange("p d x -> p (d x)"), 0.0))
                    for n in range(6):
                        s = 6 * G + n
                        for d in range(2):
                            t = TILES[d][n]
                            c0 = dec_col("ss", d, 8 * sg)
                            dve.wait_ge(spe[d].sem, spe[d].at(s, "CB"))
                            v.tensor_tensor(sCB[d], ps[4 * d + 2][:, 0:P], C[("le", "ge")[d]], ALU.mult).then_inc(sdve[d].sem, 1)
                            v.tensor_tensor(sXD[d].rearrange("p (h x) -> p h x", h=8), xt[:, t].rearrange("p (h x) -> p h x", h=8),
                                            bcast(spl[:, t, c0:c0 + 8], 64), ALU.mult).then_inc(sdve[d].sem, 1)
                        for half in range(2):
                            for d in range(2):
                                dve.wait_ge(sact[d].sem, sact[d].at(s, f"D{half}"))
                                dve.wait_ge(sdve[d].sem, sdve[d].at(s, "CBM"))
                                w = sW[d].rearrange("p (h x) -> p h x", h=4)
                                v.tensor_tensor(w, w, over(sCB[d], 4), ALU.mult).then_inc(sdve[d].sem, 1)
                        for d in range(2):
                            t = TILES[d][n]
                            c0 = dec_col("ss", d, 8 * sg)
                            dve.wait_ge(spe[d].sem, spe[d].at(s, "ST"))
                            tmp = yt[:, t] if first_visit(n) else sXD[d]
                            link(v.tensor_tensor(tmp.rearrange("p (h x) -> p h x", h=8), ps[4 * d].rearrange("p (h x) -> p h x", h=8),
                                                 bcast(EXX[:, t, 0, c0:c0 + 8], 64), ALU.mult))
                            if not first_visit(n):
                                link(v.tensor_tensor(yt[:, t], yt[:, t], tmp, ALU.add))
                            v.tensor_tensor(yt[:, t], yt[:, t], ps[4 * d + 3], ALU.add).then_inc(sdve[d].sem, 1)
                            hh = ssH[:, d].rearrange("p (h x) -> p h x", h=8)
                            link(v.tensor_tensor(hh, hh, bcast(EXX[:, t, 2, c0:c0 + 8], 64), ALU.mult))
                            v.tensor_tensor(ssH[:, d], ssH[:, d], ps[4 * d + 1], ALU.add).then_inc(sdve[d].sem, 1)
                    t0, ot0 = out_tiles(layer, sg)
                    for c in range(4):
                        j = job(layer, f"ss{sg}", 6 + c)
                        dve.wait_ge(dense_free[j % 2], free_count(j))
                    for t in range(t0, NT):
                        dve.wait_ge(ss_ot, ot0 + t - t0 + 1)
                        tk = slice(t * P, (t + 1) * P)
                        for c in range(4):
                            ins = v.scalar_tensor_tensor(out=YC[:, 4 * sg + c, tk], in0=YC[:, 4 * sg + c, tk], scalar=col(layer, "ssd", 4 * sg + c),
                                                         in1=ps[4 + t % 4][:, c * P:(c + 1) * P], op0=ALU.mult, op1=ALU.add)
                        link(ins)
                        v.tensor_tensor(YC[:, 4 * sg:4 * sg + 4, tk], YC[:, 4 * sg:4 * sg + 4, tk], szb[:, :, tk], ALU.mult).then_inc(ss_yz, 1)
                    dve.wait_ge(ss_rs, G + 1)
                    for c in range(4):
                        y = YC[:, 4 * sg + c, t0 * P:]
                        ins = v.scalar_tensor_tensor(out=y, in0=y, scalar=col(layer, "ssg", 4 * sg + c), in1=srs[:, t0 * P:], op0=ALU.mult, op1=ALU.mult)
                    ins.then_inc(ss_y, 1)
                lo, hi = (0, T) if len(segs) == 2 else (CTX, T)
                for m in range(4):
                    for br in range(3):
                        for c in range(2):
                            j = job(layer, "merge", 12 * m + 6 + 2 * br + c)
                            jg = job(layer, "merge", 12 * m + 2 * br + c)
                            dve.wait_ge(dense_free[jg % 2], free_count(jg))
                            dve.wait_ge(dense_done, j + 1)
                            dst = mt[:, 2 * m + c] if br == 0 else mtmp
                            for i, (o, w) in enumerate(segs):
                                ins = v.tensor_tensor(dst[:, o:o + w], ps[2 * (j % 2) + i][:, 0:w], gates[:, 2 * br + c, o:o + w], ALU.mult)
                            ins.then_inc(dense_free[j % 2], 1)
                            if br:
                                dve.wait_ge(dense_free[j % 2], free_count(j))
                                ins = v.tensor_tensor(mt[:, 2 * m + c, lo:hi], mt[:, 2 * m + c, lo:hi], mtmp[:, lo:hi], ALU.add)
                                if br == 2:
                                    ins.then_inc(m_ready, 1)
                                    dve.wait_ge(m_ready, KC * layer + 2 * m + c + 1)
                                else:
                                    link(ins)

                def residual(stage, part):
                    for c in range(KC):
                        j = job(layer, stage, c)
                        dve.wait_ge(dense_done, j + 1)
                        for i, (o, w) in enumerate(segs):
                            ins = v.scalar_tensor_tensor(out=X[:, c, o:o + w], in0=ps[2 * (j % 2) + i][:, 0:w], scalar=mod[:, part + c, i:i + 1],
                                                         in1=X[:, c, o:o + w], op0=ALU.mult, op1=ALU.add)
                        ins.then_inc(x_ready, 1)

                if layer == 0:
                    modulation(0, 2 * ADA0, 2 * ADA_OUT, ps[6], ADA_OUT)
                    dve.wait_ge(mod_ready, 2)
                residual("out", 16)
                if layer == 0:
                    modulation(0, 2 * ADA_OUT, 2 * ADA_P, ps[7], ADA_P)
                    dve.wait_ge(mod_ready, 3)
                norm(2 * layer + 1, segs, 1)
                for c in range(FF // P):
                    j = job(layer, "ff1", c)
                    dve.wait_ge(dense_free[j % 2], free_count(j))
                    hc = hid[:, c, lo:hi]
                    v.tensor_tensor(hc, hc, hc, ALU.mult).then_inc(hid_ready, 1)
                residual("ff2", 40)
                if layer == 0:
                    modulation(1, 0, 2 * ADA_P, ps[6], 2 * ADA_P)
                    dve.wait_ge(mod_ready, 4)

        @block.tensor
        def _(pe):
            mm, tr = nc.tensor.matmul, nc.tensor.transpose
            panel = [0]

            def slot():
                n = panel[0]
                panel[0] += 1
                pe.wait_ge(slot_full[n % RING], 16 * (n // RING + 1))
                return ring[:, n % RING * PANEL:(n % RING + 1) * PANEL]

            def dense(j, parts, segs, free=None):
                if free:
                    pe.wait_ge(*free)
                else:
                    pe.wait_ge(dense_free[j % 2], j // 2)
                for i, (o, w) in enumerate(segs):
                    for k, (wt, rows) in enumerate(parts):
                        ins = mm(ps[2 * (j % 2) + i][:, 0:w], wt, rows[:, o:o + w], start=(k == 0), stop=(k == len(parts) - 1))
                ins.then_inc(dense_done, 1)

            def from_h(j, p, c, segs):
                w = p.rearrange("p (k c) -> p k c", k=KC)
                dense(j, [(w[:, k, c * P:(c + 1) * P], H[:, k]) for k in range(KC)], segs, free_of(j))

            def free_of(j):
                r = j % NJOB
                layer = j // NJOB
                prev = j - 2
                if prev < 0:
                    return (h_ready, 1)
                rp = prev % NJOB
                lay = prev // NJOB
                if JOB_AT["out"] <= rp < JOB_AT["ff1"]:
                    return (x_ready, 2 * KC * lay + rp - JOB_AT["out"] + 1)
                if JOB_AT["ff2"] <= rp:
                    return (x_ready, 2 * KC * lay + KC + rp - JOB_AT["ff2"] + 1)
                return (dense_free[prev % 2], free_count(prev))

            def norm(q, segs):
                for k in range(KC):
                    pe.wait_ge(sq_ready, KC * q + k + 1)
                    for i, (o, w) in enumerate(segs):
                        ins = mm(ps[4 + i][:, 0:w], C["ones"], nsq[:, k % 2, o:o + w], start=(k == 0), stop=(k == KC - 1))
                    ins.then_inc(nsum_ready, 1)
                if q == 0:
                    for i in range(ADA0):
                        modulators(ada_bank, i)
                pe.wait_ge(h_ready, q + 1)

            pe.wait_ge(cst_in, 16)
            pe.wait_ge(scv_ready, 1)

            def modulators(bank, i, beside=None):
                w = slot().rearrange("p (k c) -> p k c", k=KC)
                for c in range(2):
                    if beside:
                        beside(c)
                    f = 2 * i + c
                    for k in range(KC):
                        ins = mm(bank[:, 2 * f:2 * f + 2], w[:, k, c * P:(c + 1) * P], scv[:, k], start=(k == 0), stop=(k == KC - 1))
                ins.then_inc(ada_done, 1)

            def with_modulation(beside, bank, i, work):
                if beside:
                    modulators(bank, i, work)
                else:
                    work(0)
                    work(1)

            for layer in range(DEPTH):
                segs = segs_of(layer)
                norm(2 * layer, SEGS)
                pe.wait_ge(wsm_in, 16 * (layer + 1))
                for t in range(NT):
                    for k in range(KC):
                        ins = mm(ps[6][:, t * NSM:(t + 1) * NSM], H[:, k, t * P:(t + 1) * P], wsm[:, k], start=(k == 0), stop=(k == KC - 1))
                ins.then_inc(sm_done, 1)
                pe.wait_ge(sm_dve, 2 * layer + 2)
                for t in range(NT):
                    bank, at = ps[4 + t // 3], t % 3 * 3 * NDEC
                    for e, (f, b) in enumerate((("le", "ge"), ("gt", "lt"))):
                        mm(bank[:, at + e * NDEC:at + e * NDEC + 24], C[f], dec[:, t, 0:24], start=True, stop=True)
                        mm(bank[:, at + e * NDEC + 24:at + (e + 1) * NDEC], C[b], dec[:, t, 24:48], start=True, stop=True)
                    ins = mm(bank[:, at + 2 * NDEC:at + 3 * NDEC], C["ones"], dec[:, t], start=True, stop=True)
                ins.then_inc(cum_done, 1)
                pe.wait_ge(exx_ready, layer + 1)
                blocks = na_blocks(layer)
                units = [(b, h) for b in range(len(blocks)) for h in range(4)]
                for gi in range(2):
                    G = 2 * layer + gi

                    def headsum(c):
                        pe.wait_ge(na_sq, 4 * G + c + 1)
                        if c >= 2:
                            pe.wait_ge(na_rs, 4 * G + c - 1)
                        for i, (o, w) in enumerate(SEGS):
                            ins = mm(ps[4 + 2 * (c % 2) + i][:, 0:w], C["bones"], nasq[:, c % 2, o:o + w], start=True, stop=True)
                        ins.then_inc(na_ss, 1)

                    for i in range(3):
                        p = slot()
                        for c in range(2):
                            ch = 2 * i + c
                            from_h(job(layer, f"na{gi}", ch), p, c, SEGS)
                            if 1 <= ch <= 4:
                                headsum(ch - 1)
                    pe.wait_ge(na_rs, 4 * G + 4)
                    jv = job(layer, f"na{gi}", 5)
                    pe.wait_ge(dense_free[jv % 2], free_count(jv))
                    pe.wait_ge(dense_free[(jv - 1) % 2], free_count(jv - 1))
                    for i in range(5):
                        if i == 4:
                            pe.wait_ge(na_vc, 5 * G + 1)
                        for half in range(2):
                            for c in range(2):
                                if i == 0:
                                    src = nav[:, c, half * P:(half + 1) * P]
                                else:
                                    at = CTX + window(i - 1) * GR + half * P
                                    src = nav[:, c, at:at + P]
                                ins = tr(ps[4 + i % 4][:, half * 256 + c * P:half * 256 + (c + 1) * P], src, C["ident"])
                        ins.then_inc(na_vt, 1)
                    pe.wait_ge(na_vc, 5 * G + 5)
                    pe.wait_ge(na_qk, 4 * G + 4)
                    u0 = na_u0(layer, gi)
                    b0 = u0 // 4

                    def scores(u):
                        b, h = units[u]
                        lat, i = blocks[b]
                        if u >= 3:
                            pe.wait_ge(na_P, u0 + u - 2)
                        hs = slice(64 * (h % 2), 64 * (h % 2) + 64)
                        q, k = naq[hs, h // 2], naq[hs, 2 + h // 2]
                        at = (CTX if lat else 0) + i * P
                        qs = q[:, at:at + P]
                        ins = mm(na_sbank[u % 3][:, 256:512], qs, k[:, 0:CTX], start=True, stop=True)
                        if lat:
                            ins = mm(na_sbank[u % 3][:, 0:256], qs, nak(k[:, CTX:], i), start=True, stop=True)
                        ins.then_inc(na_S, 1)

                    def back(b):
                        pe.wait_ge(na_O, b0 + b + 1)
                        if b >= 1:
                            pe.wait_ge(na_YA, b0 + b)
                        for c in range(2):
                            ins = tr(na_tbank[:, c * P:(c + 1) * P], naO[:, b % 2, c * P:(c + 1) * P], C["ident"])
                        ins.then_inc(na_OT, 1)

                    def values(u):
                        b, h = units[u]
                        lat, i = blocks[b]
                        chunks = range(4) if lat else range(2, 4)
                        pe.wait_ge(na_PT, u0 + u + 1)
                        if h == 0 and b >= 2:
                            pe.wait_ge(na_O, b0 + b - 1)
                        for n, c in enumerate(chunks):
                            tile = c - 2 if c >= 2 else 2 + 2 * i + c
                            ins = mm(na_obank[b % 2][:, h * 64:(h + 1) * 64], naPT[:, u % 2, c * P:(c + 1) * P], navt[:, tile, h * 64:(h + 1) * 64],
                                     start=(n == 0), stop=(n == len(chunks) - 1))
                        ins.then_inc(na_PV, 1)

                    scores(0)
                    scores(1)
                    for u, (b, h) in enumerate(units):
                        if u + 2 < len(units):
                            scores(u + 2)
                        lat, i = blocks[b]
                        pe.wait_ge(na_P, u0 + u + 1)
                        if u:
                            pe.wait_ge(na_PT, u0 + u)
                        for c in range(4) if lat else range(2, 4):
                            ins = tr(ps[6][:, c * P:(c + 1) * P], naP[:, u % 2, c * P:(c + 1) * P], C["ident"])
                        ins.then_inc(na_T, 1)
                        if u:
                            values(u - 1)
                        if h == 2 and b > 0:
                            back(b - 1)
                    values(len(units) - 1)
                    back(len(blocks) - 1)
                    pe.wait_ge(na_YA, b0 + len(blocks))
                for hg in range(2):
                    G = 2 * layer + hg
                    gq = 4 * layer + hg
                    for c in range(8):
                        if c % 2 == 0:
                            p = slot()
                        from_h(job(layer, f"dn{hg}", c), p, c % 2, SEGS if c < 6 else segs)
                        x = c - 2
                        if 0 <= x < 4:
                            pe.wait_ge(dq_sq, 4 * G + x + 1)
                            if x:
                                pe.wait_ge(dq_rs, 4 * G + x)
                            for i, (o, w) in enumerate(SEGS):
                                ins = mm(ps[4 + i][:, 0:w], C["bones"], sqb[:, x % 2, o:o + w], start=True, stop=True)
                            ins.then_inc(dq_ss, 1)
                        x = c - 4
                        if x >= 0:
                            pe.wait_ge(dq_n, 4 * G + x + 1)
                            if x >= 2:
                                pe.wait_ge(dq_rope, 4 * G + x - 1)
                            mm(ps[6 + x % 2][:, :], C["rot"], QK[:, x, CTX:], start=True, stop=True).then_inc(dq_rot, 1)
                    pe.wait_ge(dq_rope, 4 * G + 4)
                    pe.wait_ge(silu_done, 6 * gq + 6)
                    for t in range(NT):
                        if t >= 4:
                            pe.wait_ge(tr_copied, 6 * gq + t - 3)
                        tk = slice(t * P, (t + 1) * P)
                        for c, src in enumerate((QK[:, 2], QK[:, 3], dnV[:, 0], dnV[:, 1])):
                            ins = tr(ps[4 + t % 4][:, c * P:(c + 1) * P], src[:, tk], C["ident"])
                        ins.then_inc(tr_done, 1)
                    pe.wait_ge(tr_copied, 6 * gq + 6)
                    for z in (7, 6):
                        j = job(layer, f"dn{hg}", z)
                        pe.wait_ge(dense_free[j % 2], free_count(j))
                    hs = [slice(64 * (h % 2), 64 * (h % 2) + 64) for h in range(4)]

                    def sum_decays(s):
                        for d in range(2):
                            pe.wait_ge(dpre[d].sem, dpre[d].at(s, "R"))
                            mm(ps[4 * d + 3], C[("gt", "lt")[d]], flat(dR[d]), start=True, stop=True).then_inc(dn_seg[d], 1)

                    sum_decays(6 * G)
                    for n in range(6):
                        s = 6 * G + n
                        for qk, bank, name in ((2, 0, "VN"), (0, 2, "S")):
                            for d in range(2):
                                B = ps[4 * d:4 * d + 4]
                                tk = slice(TILES[d][n] * P, (TILES[d][n] + 1) * P)
                                if n:
                                    pe.wait_ge(ddve[d].sem, ddve[d].at(s - 1, name))
                                if bank:
                                    pe.wait_ge(dn_exp[d], s + 1)
                                for h in range(4):
                                    ins = mm(B[bank + h % 2][:, h // 2 * P:(h // 2 + 1) * P], QK[hs[h], 2 + h // 2, tk],
                                             QK[hs[h], qk + h // 2, tk], start=True, stop=True)
                                ins.then_inc(dpe[d].sem, 1)
                        for d in range(2):
                            B = ps[4 * d:4 * d + 4]
                            pe.wait_ge(ddve[d].sem, ddve[d].at(s, "XT1"))
                            for h in range(4):
                                ins = tr(B[0][:, h * P:(h + 1) * P], dXT[d][:, h], C["ident"])
                            ins.then_inc(dpe[d].sem, 1)
                        for l in LV:
                            for d in range(2):
                                B = ps[4 * d:4 * d + 4]
                                if l == 1:
                                    pe.wait_ge(dact[d].sem, dact[d].at(s, "X1"))
                                else:
                                    pe.wait_ge(ddve[d].sem, ddve[d].at(s, f"X{l - 1}"))
                                for h in range(4):
                                    ins = mm(B[0][:, h * P:(h + 1) * P], dMT[d][:, h], dX[d][:, h], start=True, stop=True)
                                ins.then_inc(dpe[d].sem, 1)
                            for d in range(2):
                                B = ps[4 * d:4 * d + 4]
                                pe.wait_ge(ddve[d].sem, ddve[d].at(s, f"Y{l}"))
                                if l > 1:
                                    pe.wait_ge(dact[d].sem, dact[d].at(s, f"XT{l - 1}"))
                                for h in range(4):
                                    c = slice(h * 64, h * 64 + 64)
                                    y = flat(dY[d])[:, c]
                                    if l < 6:
                                        ins = mm(B[1][:, c], dXT[d][:, h], y, start=True, stop=True)
                                    else:
                                        ins = mm(B[1][64 * d:64 * d + 64, c], y, dXT[d][:, h, 64 * (1 - d):64 * (1 - d) + 64], start=True, stop=True)
                                ins.then_inc(dpe[d].sem, 1)
                            if l < 6:
                                for d in range(2):
                                    B = ps[4 * d:4 * d + 4]
                                    pe.wait_ge(ddve[d].sem, ddve[d].at(s, f"X{l}"))
                                    for h in range(4):
                                        ins = tr(B[2][:, h * P:(h + 1) * P], dX[d][:, h], C["ident"])
                                    ins.then_inc(dpe[d].sem, 1)
                            if l == 3 and n < 5:
                                sum_decays(s + 1)
                        for d in range(2):
                            B = ps[4 * d:4 * d + 4]
                            pe.wait_ge(ddve[d].sem, ddve[d].at(s, "X6"))
                            pe.wait_ge(dpool[d].sem, dpool[d].at(s, "KE"))
                            for h in range(4):
                                ins = mm(B[0][hs[h], h // 2 * P:(h // 2 + 1) * P], dKE[d][:, h], dXT[d][:, h], start=True, stop=True)
                            ins.then_inc(dpe[d].sem, 1)
                        for d in range(2):
                            B = ps[4 * d:4 * d + 4]
                            t = TILES[d][n]
                            tk = slice(t * P, (t + 1) * P)
                            pe.wait_ge(dact[d].sem, dact[d].at(s, "WT"))
                            for g in range(2):
                                mm(B[1][:, g * P:(g + 1) * P], dWT[d][:, g], dnS[:, d, g], start=True, stop=False)
                                for h in (2 * g, 2 * g + 1):
                                    ins = mm(B[1][:, h * 64:h * 64 + 64], dXT[d][:, h], kvt[:, t, 256 + h * 64:256 + (h + 1) * 64],
                                             start=False, stop=h % 2 == 1)
                            ins.then_inc(dpe[d].sem, 1)
                            for g in range(2):
                                ins = mm(B[2][:, g * P:(g + 1) * P], QK[:, g, tk], dnS[:, d, g], start=True, stop=True)
                            ins.then_inc(dpe[d].sem, 1)
                        for d in range(2):
                            B = ps[4 * d:4 * d + 4]
                            pe.wait_ge(ddve[d].sem, ddve[d].at(s, "VN"))
                            if n < 5:
                                pe.wait_ge(dn_exp[d], s + 2)
                            for h in range(4):
                                ins = mm(B[3][:, h * 64:(h + 1) * 64], dAT[d][:, h], dVN[d][:, h], start=True, stop=True)
                            ins.then_inc(dpe[d].sem, 1)
                            pe.wait_ge(dpool[d].sem, dpool[d].at(s, "KD"))
                            for g in range(2):
                                ins = mm(B[3][:, 256 + g * P:256 + (g + 1) * P], flat(dKD[d])[:, g * P:(g + 1) * P], flat(dVN[d])[:, g * P:(g + 1) * P],
                                         start=True, stop=True)
                            ins.then_inc(dpe[d].sem, 1)
                    pe.wait_ge(dn_on, G + 1)
                    for c in range(2):
                        for t in range(NT):
                            bank, at = (ps[4 + 2 * c], (t - 2) * P) if t >= 2 else (ps[5 + 2 * c], t * P)
                            ins = tr(bank[:, at:at + P], dno[:, t, c * P:(c + 1) * P], C["ident"])
                    ins.then_inc(dn_ot, 1)
                    pe.wait_ge(dn_y, G + 1)
                for sg in range(2):
                    G = 2 * layer + sg
                    gq = 4 * layer + 2 + sg
                    for i in range(3):
                        p = slot()
                        for c in range(2):
                            from_h(job(layer, f"ss{sg}", 2 * i + c), p, c, SEGS)
                    pe.wait_ge(silu_done, 6 * gq + 6)
                    for t in range(NT):
                        if t >= 2:
                            pe.wait_ge(tr_copied, 6 * gq + t - 1)
                        tk = slice(t * P, (t + 1) * P)
                        for c in range(4):
                            tr(ps[4 + t % 2][:, c * P:(c + 1) * P], YC[:, 4 * sg + c, tk], C["ident"])
                        tr(ps[6 + t % 2][:, 0:P], BC[:, 0, tk], C["ident"]).then_inc(tr_done, 1)
                    pe.wait_ge(tr_copied, 6 * gq + 6)
                    for n in range(6):
                        s = 6 * G + n
                        for d in range(2):
                            B = ps[4 * d:4 * d + 4]
                            t = TILES[d][n]
                            tk = slice(t * P, (t + 1) * P)
                            pe.wait_ge(spool[d].sem, spool[d].at(s, "R0"))
                            if n:
                                pe.wait_ge(sdve[d].sem, sdve[d].at(s - 1, "H"))
                            mm(B[0], C[("gt", "lt")[d]], sR[d], start=True, stop=True).then_inc(spe[d].sem, 1)
                            mm(B[2][:, 0:P], BC[:, 0, tk], BC[:, 1, tk], start=True, stop=True).then_inc(spe[d].sem, 1)
                            pe.wait_ge(spool[d].sem, spool[d].at(s, "R1"))
                            mm(B[1], C[("gt", "lt")[d]], sR[d], start=True, stop=True).then_inc(spe[d].sem, 1)
                        for half in range(2):
                            for d in range(2):
                                B = ps[4 * d:4 * d + 4]
                                pe.wait_ge(sdve[d].sem, sdve[d].at(s, f"W{half}"))
                                for h in range(4):
                                    at = (4 * half + h) * 64
                                    ins = mm(B[3][:, at:at + 64], sW[d][:, h * P:(h + 1) * P], sXD[d][:, at:at + 64], start=True, stop=True)
                                ins.then_inc(spe[d].sem, 1)
                        for d in range(2):
                            B = ps[4 * d:4 * d + 4]
                            t = TILES[d][n]
                            tk = slice(t * P, (t + 1) * P)
                            mm(B[0], BC[:, 1, tk], ssH[:, d], start=True, stop=True).then_inc(spe[d].sem, 1)
                            pe.wait_ge(spool[d].sem, spool[d].at(s, "XW"))
                            mm(B[1], bt[:, t], sR[d], start=True, stop=True).then_inc(spe[d].sem, 1)
                    for d in range(2):
                        pe.wait_ge(sdve[d].sem, sdve[d].at(6 * G + 5, "H"))
                    t0, ot0 = out_tiles(layer, sg)
                    for t in range(t0, NT):
                        if t - t0 >= 4:
                            pe.wait_ge(ss_yz, ot0 + t - t0 - 3)
                        for c in range(4):
                            ins = tr(ps[4 + t % 4][:, c * P:(c + 1) * P], yt[:, t, c * P:(c + 1) * P], C["ident"])
                        ins.then_inc(ss_ot, 1)
                        if t == 3:
                            for i in range(2):
                                p = slot()
                                for c in range(2):
                                    from_h(job(layer, f"ss{sg}", 6 + 2 * i + c), p, c, segs)
                    for c in range(4):
                        pe.wait_ge(ss_sq, 4 * G + c + 1)
                        for i, (o, w) in enumerate(segs):
                            ins = mm(ps[4 + i][:, 0:w], C["ones"], ssq[:, c, o:o + w], start=(c == 0), stop=(c == 3))
                    ins.then_inc(ss_sum, 1)
                    pe.wait_ge(ss_rs, G + 1)
                for m in range(4):
                    beside = layer == 0 and m > 0
                    for br in range(3):
                        p = slot()
                        with_modulation(beside, ps[6], 4 * (m - 1) + br,
                                        lambda c: from_h(job(layer, "merge", 12 * m + 2 * br + c), p, c, segs))
                    pe.wait_ge(ss_y, 2 * (layer + 1))
                    w = slot().rearrange("p (k c) -> p k c", k=KC)
                    for br, Y in ((0, YA), (1, YB), (2, YC)):
                        if br == 2:
                            w = slot().rearrange("p (k c) -> p k c", k=KC)
                        for c in range(2):
                            j = job(layer, "merge", 12 * m + 6 + 2 * br + c)
                            k0, nk = (0, 4, 0)[br], (4, 4, 8)[br]
                            dense(j, [(w[:, k0 + k, c * P:(c + 1) * P], Y[:, k]) for k in range(nk)], segs, free_of(j))
                    if beside:
                        modulators(ps[6], 4 * (m - 1) + 3)
                pe.wait_ge(m_ready, KC * (layer + 1))
                for i in range(4):
                    w = slot().rearrange("p (k c) -> p k c", k=KC)

                    def project(c):
                        j = job(layer, "out", 2 * i + c)
                        dense(j, [(w[:, k, c * P:(c + 1) * P], mt[:, k]) for k in range(KC)], segs, free_of(j))

                    with_modulation(layer == 0, ps[7], i, project)
                norm(2 * layer + 1, segs)
                for i in range(FF // 256):
                    p = slot()
                    with_modulation(layer == 0, ps[6], i, lambda c: from_h(job(layer, "ff1", 2 * i + c), p, c, segs))
                pe.wait_ge(hid_ready, FF // P * (layer + 1))
                for c in range(KC):
                    parts = []
                    for half in range(2):
                        w = slot().rearrange("p (k c) -> p k c", k=16)
                        parts += [(w[:, k], hid[:, 16 * half + k]) for k in range(16)]
                    j = job(layer, "ff2", c)
                    dense(j, parts, segs, free_of(j))
                    if layer == 0:
                        modulators(ps[6], FF // 256 + c)


def _panels(w, cols=None, kc=KC, width=256):
    w = w if cols is None else w[:, cols]
    n = w.shape[1] // width
    a = w.reshape(-1, kc, P, n, width)
    return a.transpose(3, 0, 2, 1, 4).reshape(-1, P, PANEL)


def _cols(v):
    return np.asarray(v).reshape(-1, P).T


def kernel(**inputs):
    import concourse.bacc as _bacc
    from concourse.bass_utils import run_bass_kernel_spmd as _run

    a = {k: np.asarray(v) for k, v in inputs.items()}
    r = np.arange
    streams, cols, rows, small = [], [], [], []
    for l in range(DEPTH):
        w = a["w_in"][l]
        ada = [_panels(x) for x in a["w_ada"]]
        parts = [ada[0][:ADA0]] if l == 0 else []
        for g in range(2):
            parts.append(_panels(w, np.concatenate([512 * i + 256 * g + r(256) for i in range(3)])))
        for g in range(2):
            parts.append(_panels(w, np.concatenate([1536 + 512 * i + 256 * g + r(256) for i in range(4)])))
        for g in range(2):
            xbc = 4640
            parts.append(_panels(w, np.concatenate([xbc + 512 * g + r(512), xbc + 1024 + 128 * g + r(128),
                                                    xbc + 1280 + 128 * g + r(128), 3616 + 512 * g + r(512)])))
        pab = np.concatenate([a["w_pa"][l], a["w_pb"][l]], axis=0)
        for m in range(4):
            c = 256 * m + r(256)
            gate = _panels(w, np.concatenate([6208 + D * i + c for i in range(3)]))
            merge = [gate[0:1], gate[1:2], gate[2:3], np.concatenate([_panels(pab, c), _panels(a["w_pc"][l], c)])]
            for i, p in enumerate(merge):
                n = ADA0 + 4 * (m - 1) + i
                parts += [p, ada[0][n:n + 1]] if l == 0 and m else [p]
        dense = [_panels(a["w_out"][l]), _panels(a["w_ff1"][l]), _panels(a["w_ff2"][l], kc=16, width=P)]
        if l == 0:
            beside = (ada[0][ADA_OUT:], ada[1][:FF // 256], ada[1][FF // 256:])
            for p, m, n in zip(dense, beside, (1, 1, 2)):
                for i in range(len(m)):
                    parts += [p[n * i:n * i + n], m[i:i + 1]]
        else:
            parts += dense
        streams += parts
        order = np.concatenate([3584 + r(16), 3600 + r(8), 6176 + r(16), 3608 + r(8), 6192 + r(16)])
        small.append(w[:, order].reshape(KC, P, NSM).transpose(1, 0, 2))
        both = [np.concatenate([a[f"dn_{n}"][l][0], a[f"ssd_{n}"][l][0], a[f"dn_{n}"][l][1], a[f"ssd_{n}"][l][1]]) for n in ("dt_bias", "a_log")]
        rows.append(np.concatenate(both))
        cv = []
        for name, groups in (("dn_conv_w", [[2 * g, 2 * g + 1, 4 + 2 * g, 5 + 2 * g, 8 + 2 * g, 9 + 2 * g] for g in range(2)]),
                             ("ssd_conv_w", [[4 * g, 4 * g + 1, 4 * g + 2, 4 * g + 3, 8 + g, 10 + g] for g in range(2)])):
            t = a[name][l]
            for g in groups:
                for c in g:
                    cv.append(t[:, c * P:(c + 1) * P].T)
        sb_ = _cols(a["ssd_conv_b"][l])
        sscb = [sb_[:, [4 * g, 4 * g + 1, 4 * g + 2, 4 * g + 3, 8 + g, 10 + g]] for g in range(2)]
        cols.append(np.concatenate([
            _cols(a["norm1_g"][l]), _cols(a["norm2_g"][l]), *cv, *sscb,
            _cols(np.tile(a["na_q_gain"][l], 2)), _cols(np.tile(a["na_k_gain"][l], 2)), _cols(np.tile(a["dn_o_gain"][l], 2)),
            _cols(np.repeat(a["ssd_d"][l], 64)), _cols(a["ssd_o_gain"][l])], axis=1))
    rpb = np.pad(a["na_rpb"], ((0, 0), (0, 0), (0, 0), (16, 17)))
    rpb = np.stack([rpb[..., 15 - i:15 - i + BIAS_W] for i in range(BLK_C)], axis=2)
    xs = np.concatenate([a["ctx"][0], a["x"][0]], axis=0).T.reshape(KC, P, T).transpose(1, 0, 2)
    cs = np.stack([_cols(a["c"][0]), _cols(a["c_ctx"])], axis=2)
    arrays = {"x_in": xs, "c_in": cs, "stream": np.concatenate(streams), "wsmall": np.stack(small), "cols": np.stack(cols),
              "rows": np.stack(rows), "rpb": rpb, "consts": constants(),
              "bada": np.concatenate([_cols(v) for v in a["b_ada"]], axis=1)}
    arrays = {k: np.ascontiguousarray(v) for k, v in arrays.items()}
    nc = _bacc.Bacc("TRN2", target_bir_lowering=False, num_devices=1)
    args = [nc.dram_tensor(n, v.shape, F32, kind="ExternalInput").ap() for n, v in arrays.items()]
    out = nc.dram_tensor("out", (P, KC, LAT), F32, kind="ExternalOutput").ap()
    build(nc, *args, out)
    got = _run(nc, [arrays], core_ids=[0]).results[0]["out"]
    return np.ascontiguousarray(got.transpose(1, 0, 2).reshape(D, LAT).T)[None]
```
